# Optimizing a Trainium2 kernel written in Bass

```python
import jax
import jax.numpy as jnp
from jax import lax
import numpy as np

D_MODEL = 1024
BATCH = 1
SEQ = 1024
DEPTH = 1

D_LRU = 1024
LRU_BLOCKS = 4
LRU_BLOCK_W = D_LRU // LRU_BLOCKS
CONV_W = 4
LRU_C = 8.0
D_HGRN = 1024
HGRN_EXPAND = 128
HGRN_HEADS = D_HGRN // HGRN_EXPAND
HGRN_DK = HGRN_EXPAND
HGRN_DV = D_HGRN // HGRN_HEADS
CHUNK = 64
D_MIX = D_LRU + D_HGRN
D_IN = 2 * D_LRU + 4 * D_HGRN
EPS = 1e-6

kernel_name = 'hymba_style_rglru_hgrn2_block'

def rmsnorm(x, w):
    xf = x.astype(jnp.float32)
    y = xf * lax.rsqrt(jnp.mean(xf * xf, axis=-1, keepdims=True) + EPS)
    return (y * w.astype(jnp.float32)).astype(x.dtype)

def causal_depthwise_conv(x, w, b):
    seq = x.shape[1]
    xp = jnp.pad(x, ((0, 0), (CONV_W - 1, 0), (0, 0)))
    y = b
    for k in range(CONV_W):
        y = y + w[k] * xp[:, k:k + seq, :]
    return y

def rg_lru(x, w_a, b_a, w_x, b_x, lam):
    bsz, seq, _ = x.shape
    xf = x.astype(jnp.float32)
    xb = xf.reshape(bsz, seq, LRU_BLOCKS, LRU_BLOCK_W)
    r = jax.nn.sigmoid(jnp.einsum('bsnh,nhk->bsnk', xb, w_a.astype(jnp.float32)) + b_a.astype(jnp.float32)).reshape(bsz, seq, D_LRU)
    i = jax.nn.sigmoid(jnp.einsum('bsnh,nhk->bsnk', xb, w_x.astype(jnp.float32)) + b_x.astype(jnp.float32)).reshape(bsz, seq, D_LRU)
    log_a = -LRU_C * r * jax.nn.softplus(-lam.astype(jnp.float32))
    a = jnp.exp(log_a)
    u = jnp.sqrt(-jnp.expm1(2.0 * log_a)) * (i * xf)

    def combine(left, right):
        a_l, h_l = left
        a_r, h_r = right
        return a_l * a_r, a_r * h_l + h_r

    _, h = lax.associative_scan(combine, (a, u), axis=1)
    return h.astype(x.dtype)

def hgrn2_chunked(q, k, v, g):
    bsz, seq = q.shape[0], q.shape[1]
    n_chunks = seq // CHUNK

    def to_chunks(t):
        return t.reshape(bsz, n_chunks, CHUNK, HGRN_HEADS, t.shape[-1]).transpose(1, 0, 3, 2, 4)

    mask = jnp.tril(jnp.ones((CHUNK, CHUNK), dtype=bool))

    def step(state, inp):
        qc, kc, vc, gc = inp
        b = jnp.cumsum(gc, axis=2)
        o_inter = jnp.einsum('bhtk,bhkv->bhtv', qc * jnp.exp(b), state)
        diff = b[:, :, :, None, :] - b[:, :, None, :, :]
        decay = jnp.where(mask[:, :, None], jnp.exp(jnp.minimum(diff, 0.0)), 0.0)
        scores = jnp.einsum('bhtk,bhsk,bhtsk->bhts', qc, kc, decay)
        o_intra = jnp.einsum('bhts,bhsv->bhtv', scores, vc)
        b_last = b[:, :, -1:, :]
        new_state = jnp.exp(b_last[:, :, 0, :, None]) * state + jnp.einsum('bhsk,bhsv->bhkv', kc * jnp.exp(b_last - b), vc)
        return new_state, o_inter + o_intra

    s0 = jnp.zeros((bsz, HGRN_HEADS, HGRN_DK, HGRN_DV), jnp.float32)
    _, o = lax.scan(step, s0, (to_chunks(q), to_chunks(k), to_chunks(v), to_chunks(g)))
    return o.transpose(1, 0, 3, 2, 4).reshape(bsz, seq, HGRN_HEADS, HGRN_DV)

def setup_inputs(seed: int = 0) -> dict:
    key = jax.random.key(seed)
    ks = jax.random.split(key, 14)
    f32 = jnp.float32

    def nrm(k, shape, scale):
        return scale * jax.random.normal(k, shape, f32)

    x = nrm(ks[0], (BATCH, SEQ, D_MODEL), 1.0)
    pre_norm_w = 1.0 + nrm(ks[1], (DEPTH, D_MODEL), 0.05)
    w_in = nrm(ks[2], (DEPTH, D_MODEL, D_IN), D_MODEL ** -0.5)
    conv_w = nrm(ks[3], (DEPTH, CONV_W, D_LRU), CONV_W ** -0.5)
    conv_b = nrm(ks[4], (DEPTH, D_LRU), 0.01)
    lru_w_a = nrm(ks[5], (DEPTH, LRU_BLOCKS, LRU_BLOCK_W, LRU_BLOCK_W), LRU_BLOCK_W ** -0.5)
    lru_b_a = nrm(ks[6], (DEPTH, LRU_BLOCKS, LRU_BLOCK_W), 0.01)
    lru_w_x = nrm(ks[7], (DEPTH, LRU_BLOCKS, LRU_BLOCK_W, LRU_BLOCK_W), LRU_BLOCK_W ** -0.5)
    lru_b_x = nrm(ks[8], (DEPTH, LRU_BLOCKS, LRU_BLOCK_W), 0.01)
    a_pow_c = jax.random.uniform(ks[9], (DEPTH, D_LRU), f32, 0.9, 0.999)
    s = a_pow_c ** (1.0 / LRU_C)
    lru_lambda = jnp.log(s) - jnp.log1p(-s)
    hgrn_lb_logits = nrm(ks[10], (DEPTH + 1, D_HGRN), 0.1)
    hgrn_gnorm_w = 1.0 + nrm(ks[11], (DEPTH, D_HGRN), 0.05)
    w_out = nrm(ks[12], (DEPTH, D_MIX, D_MODEL), D_MIX ** -0.5)
    post_norm_w = 1.0 + nrm(ks[13], (DEPTH, D_MODEL), 0.05)
    return {'x': x, 'pre_norm_w': pre_norm_w, 'w_in': w_in, 'conv_w': conv_w, 'conv_b': conv_b,
            'lru_w_a': lru_w_a, 'lru_b_a': lru_b_a, 'lru_w_x': lru_w_x, 'lru_b_x': lru_b_x,
            'lru_lambda': lru_lambda, 'hgrn_lb_logits': hgrn_lb_logits, 'hgrn_gnorm_w': hgrn_gnorm_w,
            'w_out': w_out, 'post_norm_w': post_norm_w}

def reference(x, pre_norm_w, w_in, conv_w, conv_b, lru_w_a, lru_b_a, lru_w_x, lru_b_x,
              lru_lambda, hgrn_lb_logits, hgrn_gnorm_w, w_out, post_norm_w):
    bsz, seq, _ = x.shape
    dt = x.dtype
    f32 = jnp.float32
    lower_bounds = jnp.cumsum(jax.nn.softmax(hgrn_lb_logits.astype(f32), axis=0), axis=0)
    split_at = [D_LRU, 2 * D_LRU, 2 * D_LRU + D_HGRN, 2 * D_LRU + 2 * D_HGRN, 2 * D_LRU + 3 * D_HGRN]

    def heads(t):
        return t.reshape(bsz, seq, HGRN_HEADS, -1)

    h = x
    for layer in range(DEPTH):
        u = rmsnorm(h, pre_norm_w[layer])
        p = jnp.einsum('bsd,de->bse', u, w_in[layer])
        lru_x, lru_gate, q, f_raw, v, hgrn_gate = jnp.split(p, split_at, axis=-1)

        xc = causal_depthwise_conv(lru_x, conv_w[layer], conv_b[layer])
        y_lru = rg_lru(xc, lru_w_a[layer], lru_b_a[layer], lru_w_x[layer], lru_b_x[layer],
                       lru_lambda[layer]) * jax.nn.silu(lru_gate)

        lb = lower_bounds[layer]
        f = lb + (1.0 - lb) * jax.nn.sigmoid(f_raw.astype(f32))
        o = hgrn2_chunked(heads(jax.nn.silu(q.astype(f32))), heads(1.0 - f),
                          heads(v.astype(f32)), heads(jnp.log(f)))
        o = rmsnorm(o, hgrn_gnorm_w[layer].reshape(HGRN_HEADS, HGRN_DV)).reshape(bsz, seq, D_HGRN)
        y_hgrn = (o * jax.nn.silu(hgrn_gate.astype(f32))).astype(dt)

        y = jnp.einsum('bsm,md->bsd', jnp.concatenate([y_lru.astype(dt), y_hgrn], axis=-1), w_out[layer])
        h = h + rmsnorm(y, post_norm_w[layer]).astype(dt)
    return h


_drawn_inputs = setup_inputs


def setup_inputs(seed=0):
    import zlib

    import numpy as np

    out = dict(_drawn_inputs(seed))
    spreads = {}
    factors = {'lru_b_a': 64.0, 'lru_b_x': 49.826, 'hgrn_lb_logits': 6.672}
    for name, (base, spread) in spreads.items():
        noise = np.random.default_rng([zlib.crc32(name.encode()), seed]).standard_normal(out[name].shape)
        drawn = base * np.exp(spread * noise) if base else spread * noise
        out[name] = jnp.asarray(drawn.astype(out[name].dtype))
    for name, factor in factors.items():
        out[name] = (out[name] * factor).astype(out[name].dtype)
    return out
```

```python
from contextlib import ExitStack

import concourse.bass as bass
from concourse import mybir

F32 = mybir.dt.float32
F32R = mybir.dt.float32r
I8 = mybir.dt.int8
ALU = mybir.AluOpType
ACT = mybir.ActivationFunctionType

P = 128
EPS = 1e-6
F_FLOOR = 1e-9
M_FLOOR = 2.0 ** -60
LRU_C = 8.0
LEVELS = (64, 32, 16, 8)
SUB = 8
HALF = 512
SLOTS = 3

CW, CB, BA, BX, LAM, LB0, LB1, GN = 0, 4, 5, 6, 7, 8, 9, 10
NPAR = 11
LBC, OML, NOML, C8, NC8, TMP = 0, 1, 2, 3, 4, 5
NDER = 13

SEC_X, SEC_LG, SEC_Q, SEC_F, SEC_V, SEC_HG = range(6)
SLABS = [(SEC_F, 0), (SEC_Q, 0), (SEC_V, 0), (SEC_F, 1), (SEC_Q, 1), (SEC_V, 1),
         (SEC_X, 0), (SEC_X, 1), (SEC_HG, 0), (SEC_HG, 1), (SEC_LG, 0), (SEC_LG, 1)]
NS = len(SLABS)
SLAB = {sj: s for s, sj in enumerate(SLABS)}

WHEN = {}
for _h, _qs in enumerate([(10, 13, 15, 16, 17, 19, 20, 22, 24, 26), (27, 28, 30, 31, 32, 33, 34, 36, 38, 39)]):
    for _s, _q in zip(["tk", "tv", "u", "l0", "l1", "l2", "l3", "dg", "o", "ms"], _qs):
        WHEN.setdefault(_q, []).append((_s, _h))
for _n, _q in enumerate((40, 41, 42, 43)):
    WHEN.setdefault(_q, []).append(("g", _n))

PIECES = [(0, 6), (8, 14), (6, 8), (14, 16)]


def at(b, per, n):
    return (b + 1) * per + n


def build(nc, x, pre_norm_w, w_in, conv_w, conv_b, lru_w_a, lru_b_a, lru_w_x, lru_b_x, lru_lambda,
          hgrn_lb_logits, hgrn_gnorm_w, w_out, post_norm_w, out, y_scr):
    T, D = x.shape[1], x.shape[2]
    NT, KD, MT = T // P, D // P, w_out.shape[1] // P
    NB, NC = KD // 2, T // P
    assert T == 1024 and D == 1024 and MT == 2 * KD

    ctx = ExitStack()
    with ctx:
        def sem(name):
            return ctx.enter_context(nc.semaphore(name))

        def sb(name, shape, dt=F32, c=ctx):
            return c.enter_context(nc.sbuf_tensor(name, shape, dt))

        ident = sb("ident", [P, P])
        ones = sb("ones", [P, P])
        maskl = [sb(f"mask{l}", [P, 1, P // (2 * l), l], I8) for l in LEVELS]
        maskd = sb("maskd", [P, 1, P], I8)
        keep = sb("keep", [P, T], I8)
        eps_c = sb("eps_c", [P, 1])
        mfl_c = sb("mfl_c", [P, 1])
        par = sb("par", [P, NPAR, KD])
        der = sb("der", [P, NDER, KD])
        dec = sb("dec", [P, NC])
        ssq = sb("ssq", [P, NT])
        rst = sb("rst", [P, NT])
        gate = sb("gate", [1, 1])

        prod = [ctx.enter_context(nc.psum_tensor(f"prod{i}", [P, T], F32)) for i in range(2)]
        mix = [ctx.enter_context(nc.psum_tensor(f"mix{i}", [P, T], F32)) for i in range(2)]

        c_pool, c_const, p_land, p_T, p_par, p_dve, p_act, pw_land = [sem(n) for n in (
            "c_pool c_const p_land p_T p_par p_dve p_act pw_land").split()]
        x_land = [sem(f"x_land{i}") for i in range(4)]
        x_ssq, x_ln, x_rst, x_scaled, x_tr, u_hi, u_lo = [sem(n) for n in (
            "x_ssq x_ln x_rst x_scaled x_tr u_hi u_lo").split()]
        w_land = [sem(f"w_land{i}") for i in range(2)]
        wx_land = [sem(f"wx_land{i}") for i in range(2)]
        g_land = [sem(f"g_land{i}") for i in range(2)]
        w_hi, w_lo, slab = sem("w_hi"), sem("w_lo"), sem("slab")
        sf_r, sq_r, v_r, lf_r, k_r, b_r, q_r = [sem(n) for n in "sf_r sq_r v_r lf_r k_r b_r q_r".split()]
        d_r, e_r, x_r, dec_r = [sem(n) for n in "d_r e_r x_r dec_r".split()]
        pe_tk, pe_tv, pe_u, pe_l, pe_dg, pe_o, pe_ms, pe_g = [sem(n) for n in (
            "pe_tk pe_tv pe_u pe_l pe_dg pe_o pe_ms pe_g").split()]
        kt_r, vt_r, st_r, sc_r, o2_r, ln_r, rs_r, z_r = [sem(n) for n in "kt_r vt_r st_r sc_r o2_r ln_r rs_r z_r".split()]
        shg_r, hg_r, y_r = [sem(n) for n in "shg_r hg_r y_r".split()]
        xt_r, cv_r, r_r, i_r, th_r, a_r, a2_r, m2_r, ml_r, m_r = [sem(n) for n in (
            "xt_r cv_r r_r i_r th_r a_r a2_r m2_r ml_r m_r").split()]
        ix_r, lu_r, h_r, slg_r, lg_r, yl_r = [sem(n) for n in "ix_r lu_r h_r slg_r lg_r yl_r".split()]
        yh_st = [sem(f"yh_st{i}") for i in range(2)]
        yl_st = sem("yl_st")

        PER_PE = {slab: NS, pe_tk: 2, pe_tv: 2, pe_u: 2, pe_l: 8, pe_dg: 2, pe_o: 2, pe_ms: 2, pe_g: 4}
        PER_ACT = {w_hi: NS, sf_r: 2, sq_r: 2, v_r: 2, lf_r: 2, e_r: 16, dec_r: 2, kt_r: 2, vt_r: 2, o2_r: 2, ln_r: 2, rs_r: 2,
                   shg_r: 2, xt_r: 2, r_r: 2, i_r: 2, th_r: 2, a_r: 2, a2_r: 2, ml_r: 2, m_r: 2, slg_r: 2, yl_st: 32}
        PER_DVE = {k_r: 2, b_r: 2, q_r: 2, d_r: 12, x_r: 16, st_r: 14, sc_r: 10, z_r: 2, hg_r: 2, y_r: 2,
                   cv_r: 6, m2_r: 2, ix_r: 2, lu_r: 2, h_r: 2, lg_r: 2, yl_r: 2}
        PER_POOL = {w_lo: NS}
        PER_SP = {yh_st[0]: 16, yh_st[1]: 16}

        def start_full(eng, per):
            for s, n in per.items():
                eng.sem_inc(s, n)

        with ExitStack() as mctx:
            def mb(name, shape, dt=F32):
                return mctx.enter_context(nc.sbuf_tensor(name, shape, dt))

            uhi = mb("uhi", [P, KD, T], F32R)
            ulo = mb("ulo", [P, KD, T], F32R)
            whi = [mb(f"whi{i}", [P, KD, P], F32R) for i in range(SLOTS)]
            wlo = [mb(f"wlo{i}", [P, KD, P], F32R) for i in range(SLOTS)]
            wraw = [mb(f"wraw{i}", [P, KD, P]) for i in range(2)]
            gw = mb("gw", [P, 2, 2, 2 * P])
            K = [mb(f"K{h}", [P, T]) for h in range(2)]
            Q = [mb(f"Q{h}", [P, T]) for h in range(2)]
            V = [mb(f"V{h}", [P, T]) for h in range(2)]
            XC = [mb(f"XC{h}", [P, T]) for h in range(2)]
            Bs = mb("Bs", [P, T])
            QE = mb("QE", [P, T])
            S = mb("S", [P, NC, P])
            ST = mb("ST", [P, NC, P])
            Dt = [mb(f"D{i}", [P, T]) for i in range(2)]
            Et = [mb(f"E{i}", [P, T]) for i in range(2)]
            KE = mb("KE", [P, T])
            X4 = [mb(f"X{i}", [P, T]) for i in range(4)]
            R, I, G, SG = mb("R", [P, T]), mb("I", [P, T]), mb("G", [P, T]), mb("SG", [P, T])
            xstage = [R, I, Bs, QE]
            pwb, prow = XC[0], XC[1]

            x_v = x[0].rearrange("(t p) d -> t p d", p=P)
            w_v = w_in[0].rearrange("(k p) (s j c) -> p k s j c", p=P, s=6, c=P)
            ga_v = lru_w_a[0].rearrange("n (k p) c -> p n k c", p=P)
            gx_v = lru_w_x[0].rearrange("n (k p) c -> p n k c", p=P)
            y_v = y_scr.rearrange("m p t -> p m t")

            def col(table, row, j):
                return table[:, row, bass.ds(j, 1)]

            def chunks(t_, w=P):
                return t_[:].rearrange("p (c t) -> p c t", t=w)

            def known(eng, v):
                return v if isinstance(v, int) else eng.snap(v)

            with nc.Block() as blk:
                @blk.sync
                def _(sp):
                    start_full(sp, PER_SP)
                    rows = [(conv_w[0].rearrange("k (j p) -> (k j) p", p=P), 4 * KD),
                            (conv_b.rearrange("a (j p) -> (a j) p", p=P), KD),
                            (lru_b_a[0].rearrange("n (j p) -> (n j) p", p=P), KD),
                            (lru_b_x[0].rearrange("n (j p) -> (n j) p", p=P), KD),
                            (lru_lambda.rearrange("a (j p) -> (a j) p", p=P), KD),
                            (hgrn_lb_logits.rearrange("a (j p) -> (a j) p", p=P), 2 * KD),
                            (hgrn_gnorm_w.rearrange("a (j p) -> (a j) p", p=P), KD)]
                    sp.dma_start(xstage[0][:], x_v[0]).then_inc(x_land[0], 16)
                    sp.dma_start(pwb[:], pre_norm_w.to_broadcast([P, D])).then_inc(pw_land, 16)
                    for t in range(1, 4):
                        sp.dma_start(xstage[t][:], x_v[t]).then_inc(x_land[t], 16)
                    n = 0
                    for src, cnt in rows:
                        sp.dma_start(prow[n:n + cnt, 0:P], src).then_inc(p_land, 16)
                        n += cnt
                    for s in range(2):
                        sec, j = SLABS[s]
                        sp.dma_start(wraw[s][:], w_v[:, :, sec, j, :]).then_inc(w_land[s], 16)
                    for t in range(4, NT):
                        sp.wait_ge(x_tr, t - 3)
                        sp.dma_start(xstage[t % 4][:], x_v[t]).then_inc(x_land[t % 4], 16)

                    def load_block(b, last):
                        for k in range(2, NS if last else NS + 2):
                            sec, j = SLABS[k % NS]
                            if sec == SEC_X:
                                continue
                            jj = b * 2 + j + (2 if k >= NS else 0)
                            need = known(sp, at(b, NS, k - 1))
                            sp.wait_ge(w_lo, need)
                            sp.dma_start(wraw[k % 2][:], w_v[:, :, sec, bass.ds(jj, 1), :].rearrange("p k j c -> p k (j c)")
                                         ).then_inc(w_land[k % 2], 16)
                            if k in (3, 4):
                                src = (ga_v, gx_v)[k - 3]
                                bb = known(sp, b + 0)
                                need = known(sp, at(b, 4, 0))
                                sp.wait_ge(pe_g, need)
                                sp.dma_start(gw[:, k - 3], src[:, bass.ds(bb, 1)].rearrange("p n k c -> p (n k) c")
                                             ).then_inc(g_land[k - 3], 16)
                        for h in range(2):
                            m = known(sp, b * 2 + h + KD)
                            need = known(sp, at(b, 2, h + 1))
                            sp.wait_ge(y_r, need)
                            sp.dma_start(y_v[:, bass.ds(m, 1), :].rearrange("p m t -> p (m t)"), V[h][:]).then_inc(yh_st[h], 16)

                    with sp.Fori(0, NB - 1) as b:
                        load_block(b, False)
                    load_block(NB - 1, True)
                    for h in range(2):
                        sp.wait_ge(yh_st[h], at(NB, 16, 0))

                @blk.gpsimd
                def _(pool):
                    start_full(pool, PER_POOL)
                    n = [0]

                    def step(ins):
                        n[0] += 1
                        ins.then_inc(c_pool, 1)
                        pool.wait_ge(c_pool, n[0])

                    step(pool.memset(ident[:], 0.0))
                    step(pool.affine_select(out=ident[:], in_=ident[:], compare_op=ALU.not_equal, fill=1.0, base=0,
                                            pattern=[[-1, P]], channel_multiplier=1))
                    step(pool.memset(eps_c[:], EPS))
                    pool.memset(ones[:], 1.0 / P)
                    pool.memset(mfl_c[:], M_FLOOR)
                    pool.memset(S[:], 0.0)
                    step(pool.memset(keep[:], 1))
                    step(pool.memset(keep[:].rearrange("p (c t) -> p c t", t=P)[:, :, 0:1], 0))
                    for l, m in zip(LEVELS, maskl):
                        mm = m[:, 0]
                        step(pool.memset(m[:], 1))
                        step(pool.affine_select(out=mm, in_=mm, compare_op=ALU.is_ge, fill=0, base=0,
                                                pattern=[[-2 * l, P // (2 * l)], [0, l]], channel_multiplier=1))
                        step(pool.affine_select(out=mm, in_=mm, compare_op=ALU.is_ge, fill=0, base=l - 1,
                                                pattern=[[2 * l, P // (2 * l)], [0, l]], channel_multiplier=-1))
                    md = maskd[:, 0].rearrange("p (i t) -> p i t", t=SUB)
                    step(pool.memset(maskd[:], 1))
                    step(pool.affine_select(out=md, in_=md, compare_op=ALU.is_ge, fill=0, base=0,
                                            pattern=[[-SUB, P // SUB], [0, SUB]], channel_multiplier=1))
                    pool.affine_select(out=md, in_=md, compare_op=ALU.is_ge, fill=0, base=0,
                                       pattern=[[SUB, P // SUB], [1, SUB]], channel_multiplier=-1).then_inc(c_const, 1)

                    def low_parts(b, ks):
                        for k in ks:
                            pool.wait_ge(w_hi, at(b, NS, k + 1))
                            pool.tensor_tensor(wlo[k % SLOTS][:], wraw[k % 2][:], whi[k % SLOTS][:],
                                               ALU.subtract).then_inc(w_lo, 1)
                            sec, j = SLABS[(k + 2) % NS]
                            if sec == SEC_X:
                                pool.wait_ge(w_lo, at(b, NS, k + 1))
                                pool.dma_start(wraw[k % 2][:], w_v[:, :, sec, bass.ds(b * 2 + j, 1), :].rearrange(
                                    "p k j c -> p k (j c)")).then_inc(wx_land[j], 16)

                    low_parts(0, range(3))
                    with pool.Fori(0, NB - 1) as b:
                        low_parts(b, range(3, NS + 3))
                    low_parts(NB - 1, range(3, NS))

                @blk.scalar
                def _(act):
                    start_full(act, PER_ACT)
                    A = nc.scalar.activation

                    def high_part(b, k):
                        sec, j = SLABS[k % NS]
                        if sec == SEC_X:
                            act.wait_ge(wx_land[j], b * 16 + 16)
                        else:
                            before = sum(s % 2 == k % 2 and SLABS[s][0] != SEC_X for s in range(k % NS))
                            act.wait_ge(w_land[k % 2], (b + k // NS) * 80 + (before + 1) * 16)
                        act.wait_ge(slab, at(b, NS, k - 2))
                        A(whi[k % SLOTS][:], wraw[k % 2][:], ACT.Copy).then_inc(w_hi, 1)

                    for t in range(NT):
                        act.wait_ge(x_land[t % 4], 16 * (t // 4 + 1))
                        if t >= 1:
                            act.wait_ge(x_ssq, t)
                        A(Et[0][:], xstage[t % 4][:], ACT.Square, accum_out=ssq[:, t:t + 1]).then_inc(x_ssq, 1)
                        act.wait_ge(x_ssq, t + 1)
                        act.wait_ge(c_pool, 3)
                        A(rst[:, t:t + 1], ssq[:, t:t + 1], ACT.Ln, scale=1.0 / D, bias=eps_c[:]).then_inc(x_ln, 1)
                        act.wait_ge(x_ln, t + 1)
                        A(rst[:, t:t + 1], rst[:, t:t + 1], ACT.Exp, scale=-0.5).then_inc(x_rst, 1)
                        if 2 <= t < 4:
                            high_part(0, t - 2)
                        if t >= 1:
                            act.wait_ge(x_tr, t)
                            A(uhi[:, :, (t - 1) * P:t * P], chunks(mix[(t - 1) % 2]), ACT.Copy).then_inc(u_hi, 1)
                    act.wait_ge(x_tr, NT)
                    A(uhi[:, :, T - P:], chunks(mix[(NT - 1) % 2]), ACT.Copy).then_inc(u_hi, 1)
                    act.wait_ge(p_dve, 4)
                    A(der[:, TMP + 0], der[:, TMP + 0], ACT.Exp).then_inc(p_act, 1)
                    A(der[:, TMP + 1], der[:, TMP + 1], ACT.Exp).then_inc(p_act, 1)
                    A(der[:, TMP + 2], der[:, TMP + 2], ACT.Exp, scale=-1.0).then_inc(p_act, 1)
                    high_part(0, 2)
                    act.wait_ge(p_par, 1)
                    act.wait_ge(c_const, 1)

                    def forget_gate(b, h):
                        s = SLAB[SEC_F, h]
                        act.wait_ge(slab, at(b, NS, s + 1))
                        act.wait_ge(x_r, at(b, 16, 8 * h - 9))
                        A(K[h][:], prod[s % 2][:], ACT.Sigmoid).then_inc(sf_r, 1)

                    def log_f(b, h):
                        act.wait_ge(sf_r, at(b, 2, h + 1))
                        act.wait_ge(e_r, at(b, 16, 8 * h))
                        A(Bs[:], K[h][:], ACT.Ln, scale=col(der, OML, b * 2 + h),
                          bias=col(der, LBC, b * 2 + h)).then_inc(lf_r, 1)

                    def exps(b, h, n):
                        e = Et[(n - 1) % 2]
                        if n == 8:
                            act.wait_ge(b_r, at(b, 2, h + 1))
                        else:
                            act.wait_ge(d_r, at(b, 12, 6 * h + min(n, 6)))
                        act.wait_ge(x_r, at(b, 16, 8 * h + n - 2))
                        if 2 <= n <= 5:
                            l = LEVELS[n - 2]
                            dv, ev = chunks(Dt[(n - 1) % 2], 2 * l), chunks(e, 2 * l)
                            A(ev[:, :, 0:l], dv[:, :, 0:l], ACT.Exp, scale=-1.0)
                            A(ev[:, :, l:], dv[:, :, l:], ACT.Exp).then_inc(e_r, 1)
                        elif n == 8:
                            A(e[:], Bs[:], ACT.Exp).then_inc(e_r, 1)
                        else:
                            A(e[:], Dt[(min(n, 6) - 1) % 2][:], ACT.Exp, scale=1.0 if n == 6 else -1.0).then_inc(e_r, 1)

                    def chunk_decay(b, h):
                        act.wait_ge(b_r, at(b, 2, h + 1))
                        act.wait_ge(st_r, at(b, 14, 7 * h))
                        A(dec[:], chunks(Bs)[:, :, P - 1], ACT.Exp).then_inc(dec_r, 1)

                    def query_gate(b, h):
                        s = SLAB[SEC_Q, h]
                        act.wait_ge(slab, at(b, NS, s + 1))
                        act.wait_ge(y_r, at(b, 2, h - 1))
                        A(Q[h][:], prod[s % 2][:], ACT.Sigmoid).then_inc(sq_r, 1)

                    def values(b, h):
                        s = SLAB[SEC_V, h]
                        act.wait_ge(slab, at(b, NS, s + 1))
                        act.wait_ge(yh_st[h], at(b, 16, 0))
                        A(V[h][:], prod[s % 2][:], ACT.Copy).then_inc(v_r, 1)

                    def keys_by_token(b, h):
                        act.wait_ge(pe_tk, at(b, 2, h + 1))
                        A(KE[:], mix[0][:], ACT.Copy).then_inc(kt_r, 1)

                    def values_by_token(b, h):
                        act.wait_ge(pe_tv, at(b, 2, h + 1))
                        A(V[h][:], mix[1][:], ACT.Copy).then_inc(vt_r, 1)

                    def square_out(b, h):
                        act.wait_ge(pe_o, at(b, 2, h + 1))
                        act.wait_ge(z_r, at(b, 2, h))
                        act.wait_ge(lu_r, at(b, 2, 0))
                        A(G[:], mix[0][:], ACT.Square).then_inc(o2_r, 1)

                    def head_rstd(b, h):
                        act.wait_ge(pe_ms, at(b, 2, h + 1))
                        A(G[:], mix[1][:], ACT.Ln, bias=eps_c[:]).then_inc(ln_r, 1)
                        act.wait_ge(ln_r, at(b, 2, h + 1))
                        A(G[:], G[:], ACT.Exp, scale=-0.5).then_inc(rs_r, 1)

                    def head_gate(b, h):
                        s = SLAB[SEC_HG, h]
                        act.wait_ge(slab, at(b, NS, s + 1))
                        act.wait_ge(pe_o, at(b, 2, h + 1))
                        A(V[h][:], prod[s % 2][:], ACT.Sigmoid).then_inc(shg_r, 1)

                    def first_tap(b, i):
                        s = SLAB[SEC_X, i]
                        act.wait_ge(slab, at(b, NS, s + 1))
                        act.wait_ge(yl_r, at(b, 2, i - 1))
                        A(XC[i][:], prod[s % 2][:], ACT.Identity, scale=col(par, CW + 3, b * 2 + i),
                          bias=col(par, CB, b * 2 + i)).then_inc(xt_r, 1)

                    def lru_gates(b, i):
                        act.wait_ge(pe_g, at(b, 4, 2 * i + 1))
                        act.wait_ge(h_r, at(b, 2, i))
                        A(R[:], mix[0][:], ACT.Sigmoid, bias=col(par, BA, b * 2 + i)).then_inc(r_r, 1)
                        act.wait_ge(pe_g, at(b, 4, 2 * i + 2))
                        A(I[:], mix[1][:], ACT.Sigmoid, bias=col(par, BX, b * 2 + i)).then_inc(i_r, 1)
                        act.wait_ge(r_r, at(b, 2, i + 1))
                        act.wait_ge(z_r, at(b, 2, 2))
                        act.wait_ge(lu_r, at(b, 2, i))
                        A(G[:], R[:], ACT.Tanh, scale=col(der, C8, b * 2 + i)).then_inc(th_r, 1)

                    def lru_decay(b, i):
                        act.wait_ge(th_r, at(b, 2, i + 1))
                        A(R[:], R[:], ACT.Exp, scale=col(der, NC8, b * 2 + i)).then_inc(a_r, 1)
                        act.wait_ge(a_r, at(b, 2, i + 1))
                        if i == 0:
                            act.wait_ge(yl_st, at(b, 32, 0))
                        else:
                            act.wait_ge(m2_r, at(b, 2, 1))
                        A(SG[:], R[:], ACT.Square).then_inc(a2_r, 1)
                        act.wait_ge(m2_r, at(b, 2, i + 1))
                        A(G[:], G[:], ACT.Ln, bias=mfl_c[:]).then_inc(ml_r, 1)
                        act.wait_ge(ml_r, at(b, 2, i + 1))
                        A(G[:], G[:], ACT.Exp, scale=0.5).then_inc(m_r, 1)

                    def lru_gate(b, i):
                        s = SLAB[SEC_LG, i]
                        act.wait_ge(slab, at(b, NS, s + 1))
                        if i == 0:
                            act.wait_ge(m2_r, at(b, 2, 2))
                        else:
                            act.wait_ge(yl_st, at(b, 32, 16))
                        A(SG[:], prod[s % 2][:], ACT.Sigmoid).then_inc(slg_r, 1)

                    def store_lru(b, i):
                        m = known(act, b * 2 + i)
                        act.wait_ge(yl_r, at(b, 2, i + 1))
                        act.dma_start(y_v[:, bass.ds(m, 1), :].rearrange("p m t -> p (m t)"), SG[:]).then_inc(yl_st, 16)

                    def block_act(b, last):
                        forget_gate(b, 0); high_part(b, 3)
                        log_f(b, 0)
                        exps(b, 0, 1); exps(b, 0, 2); chunk_decay(b, 0)
                        query_gate(b, 0); high_part(b, 4)
                        keys_by_token(b, 0)
                        exps(b, 0, 3)
                        values(b, 0); high_part(b, 5)
                        exps(b, 0, 4)
                        values_by_token(b, 0)
                        exps(b, 0, 5); exps(b, 0, 6)
                        forget_gate(b, 1); high_part(b, 6)
                        exps(b, 0, 7); exps(b, 0, 8)
                        log_f(b, 1)
                        query_gate(b, 1); high_part(b, 7)
                        exps(b, 1, 1); exps(b, 1, 2); chunk_decay(b, 1)
                        values(b, 1); high_part(b, 8)
                        square_out(b, 0)
                        exps(b, 1, 3)
                        head_rstd(b, 0)
                        exps(b, 1, 4)
                        first_tap(b, 0); high_part(b, 9)
                        keys_by_token(b, 1)
                        values_by_token(b, 1)
                        exps(b, 1, 5); exps(b, 1, 6); exps(b, 1, 7); exps(b, 1, 8)
                        first_tap(b, 1); high_part(b, 10)
                        head_gate(b, 0); high_part(b, 11)
                        square_out(b, 1)
                        head_rstd(b, 1)
                        head_gate(b, 1)
                        if not last:
                            high_part(b, 12)
                        lru_gates(b, 0)
                        lru_decay(b, 0)
                        lru_gates(b, 1)
                        lru_decay(b, 1)
                        lru_gate(b, 0)
                        if not last:
                            high_part(b, 13)
                        store_lru(b, 0)
                        lru_gate(b, 1)
                        if not last:
                            high_part(b, 14)
                        store_lru(b, 1)

                    with act.Fori(0, NB - 1) as b:
                        block_act(b, False)
                    block_act(NB - 1, True)
                    act.wait_ge(yl_st, at(NB, 32, 0))

                @blk.vector
                def _(dve):
                    start_full(dve, PER_DVE)
                    V_ = nc.vector
                    TT, TS, STT = V_.tensor_tensor, V_.tensor_scalar, V_.scalar_tensor_tensor

                    for t in range(NT):
                        if t == 0:
                            dve.wait_ge(pw_land, 16)
                        dve.wait_ge(x_rst, t + 1)
                        STT(out=xstage[t % 4][:], in0=xstage[t % 4][:], scalar=rst[:, t:t + 1], in1=pwb[:],
                            op0=ALU.mult, op1=ALU.mult).then_inc(x_scaled, 1)
                        if t >= 1:
                            dve.wait_ge(u_hi, t)
                            TT(ulo[:, :, (t - 1) * P:t * P], chunks(mix[(t - 1) % 2]), uhi[:, :, (t - 1) * P:t * P],
                               ALU.subtract).then_inc(u_lo, 1)
                    dve.wait_ge(u_hi, NT)
                    TT(ulo[:, :, T - P:], chunks(mix[(NT - 1) % 2]), uhi[:, :, T - P:], ALU.subtract).then_inc(u_lo, 1)

                    n = [0]

                    def step(ins):
                        n[0] += 1
                        ins.then_inc(p_dve, 1)
                        dve.wait_ge(p_dve, n[0])

                    def tmp(i):
                        return der[:, TMP + i]

                    dve.wait_ge(p_T, 1)
                    step(V_.tensor_copy(par[:], prod[1][:, 0:NPAR * KD].rearrange("p (r j) -> p r j", j=KD)))
                    TT(tmp(3), par[:, LB0], par[:, LB1], ALU.max).then_inc(p_dve, 1)
                    n[0] += 1
                    step(TS(tmp(4), par[:, LAM], -1.0, None, ALU.mult))
                    TT(tmp(0), par[:, LB0], tmp(3), ALU.subtract)
                    TT(tmp(1), par[:, LB1], tmp(3), ALU.subtract)
                    step(TT(tmp(2), par[:, LAM], tmp(4), ALU.max))
                    dve.wait_ge(p_act, 3)
                    step(TT(tmp(3), tmp(0), tmp(1), ALU.add))
                    step(V_.reciprocal(tmp(3), tmp(3)))
                    TT(der[:, LBC], tmp(0), tmp(3), ALU.mult)
                    step(TT(der[:, OML], tmp(1), tmp(3), ALU.mult))
                    step(TS(der[:, LBC], der[:, LBC], F_FLOOR, None, ALU.max))
                    step(TS(der[:, NOML], der[:, OML], -1.0, None, ALU.mult))
                    step(TS(tmp(5), tmp(2), 2.0, None, ALU.add))
                    step(V_.reciprocal(tmp(5), tmp(5)))
                    step(TT(tmp(5), tmp(5), tmp(2), ALU.mult))
                    step(TT(tmp(6), tmp(5), tmp(5), ALU.mult))
                    step(TS(tmp(7), tmp(6), 1.0 / 19, 1.0 / 17, ALU.mult, ALU.add))
                    for k in range(15, 0, -2):
                        step(TT(tmp(7), tmp(7), tmp(6), ALU.mult))
                        step(TS(tmp(7), tmp(7), 1.0 / k, None, ALU.add))
                    step(TT(tmp(7), tmp(7), tmp(5), ALU.mult))
                    step(TS(tmp(4), tmp(4), 0.0, LRU_C, ALU.max, ALU.mult))
                    step(STT(out=der[:, C8], in0=tmp(7), scalar=2.0 * LRU_C, in1=tmp(4), op0=ALU.mult, op1=ALU.add))
                    step(TS(der[:, NC8], der[:, C8], -1.0, None, ALU.mult))
                    dve.wait_ge(c_const, 1)
                    V_.memset(gate[:], 0.0).then_inc(p_par, 1)

                    def key(b, h):
                        dve.wait_ge(lf_r, at(b, 2, h + 1))
                        TS(K[h][:], K[h][:], col(der, NOML, b * 2 + h), col(der, OML, b * 2 + h),
                           ALU.mult, ALU.add).then_inc(k_r, 1)
                        V_.tensor_tensor_scan(Bs[:], keep[:], Bs[:], 0.0, ALU.mult, ALU.add).then_inc(b_r, 1)

                    def diff(b, h, j):
                        w, ref = {1: (P, P - 1), 6: (SUB, SUB // 2 - 1)}.get(j) or (2 * LEVELS[j - 2], LEVELS[j - 2] - 1)
                        dve.wait_ge(b_r, at(b, 2, h + 1))
                        dve.wait_ge(e_r, at(b, 16, 8 * h + {1: -3, 2: -1}.get(j, j - 2)))
                        bv = chunks(Bs, w)
                        TT(chunks(Dt[(j - 1) % 2], w), bv, bv[:, :, ref:ref + 1].to_broadcast([P, T // w, w]),
                           ALU.subtract).then_inc(d_r, 1)

                    def prod_e(b, h, n):
                        e = Et[(n - 1) % 2]
                        dve.wait_ge(e_r, at(b, 16, 8 * h + n))
                        if n == 1:
                            dve.wait_ge(k_r, at(b, 2, h + 1))
                            dve.wait_ge(pe_u, at(b, 2, h))
                            TT(KE[:], K[h][:], e[:], ALU.mult).then_inc(x_r, 1)
                        elif n <= 5:
                            l = LEVELS[n - 2]
                            dve.wait_ge(q_r, at(b, 2, h + 1))
                            dve.wait_ge(pe_dg, at(b, 2, h))
                            xv, ev = chunks(X4[n - 2], 2 * l), chunks(e, 2 * l)
                            TT(xv[:, :, 0:l], chunks(K[h], 2 * l)[:, :, 0:l], ev[:, :, 0:l], ALU.mult)
                            TT(xv[:, :, l:], chunks(Q[h], 2 * l)[:, :, l:], ev[:, :, l:], ALU.mult).then_inc(x_r, 1)
                        elif n <= 7:
                            dve.wait_ge(pe_l, at(b, 8, 4 * h + n - 5))
                            TT(X4[n - 6][:], (Q, K)[n - 6][h][:], e[:], ALU.mult).then_inc(x_r, 1)
                        else:
                            dve.wait_ge(pe_o, at(b, 2, h))
                            TT(QE[:], Q[h][:], e[:], ALU.mult).then_inc(x_r, 1)

                    def query(b, h):
                        dve.wait_ge(sq_r, at(b, 2, h + 1))
                        TT(Q[h][:], Q[h][:], prod[SLAB[SEC_Q, h] % 2][:], ALU.mult).then_inc(q_r, 1)

                    def states(b, h):
                        dve.wait_ge(pe_u, at(b, 2, h + 1))
                        dve.wait_ge(pe_o, at(b, 2, h))
                        dve.wait_ge(dec_r, at(b, 2, h + 1))
                        V_.tensor_copy(ST[:, 1], mix[0][:, 0:P]).then_inc(st_r, 1)
                        for c in range(1, NC - 1):
                            dve.wait_ge(st_r, at(b, 14, 7 * h + c))
                            STT(out=ST[:, c + 1], in0=ST[:, c], scalar=dec[:, c:c + 1], in1=mix[0][:, c * P:(c + 1) * P],
                                op0=ALU.mult, op1=ALU.add).then_inc(st_r, 1)

                    def scores(b, h, i):
                        dve.wait_ge(sc_r, at(b, 10, 5 * h + i))
                        if i == 0:
                            dve.wait_ge(pe_o, at(b, 2, h))
                        if i < 4:
                            dve.wait_ge(pe_l, at(b, 8, 4 * h + i + 1))
                        else:
                            dve.wait_ge(pe_dg, at(b, 2, h + 1))
                        V_.memset(gate[:], 0.0)
                        m = mix[(1, 0, 1, 0, 1)[i]]
                        if i < 4:
                            l = LEVELS[i]
                            nb = P // (2 * l)
                            V_.copy_predicated(S[:].rearrange("p c (i t) -> p c i t", t=2 * l)[:, :, :, l:],
                                               maskl[i][:].to_broadcast([P, NC, nb, l]),
                                               m[:, 0:HALF].rearrange("p (c i t) -> p c i t", c=NC, t=l)).then_inc(sc_r, 1)
                        else:
                            V_.copy_predicated(S[:], maskd[:].to_broadcast([P, NC, P]), chunks(m)).then_inc(sc_r, 1)

                    def norm(b, h):
                        dve.wait_ge(rs_r, at(b, 2, h + 1))
                        dve.wait_ge(x_r, at(b, 16, 8 * h + 8))
                        STT(out=Q[h][:], in0=mix[0][:], scalar=col(par, GN, b * 2 + h), in1=G[:],
                            op0=ALU.mult, op1=ALU.mult).then_inc(z_r, 1)

                    def head_out(b, h):
                        dve.wait_ge(shg_r, at(b, 2, h + 1))
                        TT(V[h][:], V[h][:], prod[SLAB[SEC_HG, h] % 2][:], ALU.mult).then_inc(hg_r, 1)
                        dve.wait_ge(hg_r, at(b, 2, h + 1))
                        dve.wait_ge(z_r, at(b, 2, h + 1))
                        TT(V[h][:], V[h][:], Q[h][:], ALU.mult).then_inc(y_r, 1)

                    def conv(b, i):
                        dve.wait_ge(xt_r, at(b, 2, i + 1))
                        src = prod[SLAB[SEC_X, i] % 2]
                        for d in range(1, 4):
                            if d > 1:
                                dve.wait_ge(cv_r, at(b, 6, 3 * i + d - 1))
                            STT(out=XC[i][:, d:], in0=src[:, 0:T - d], scalar=col(par, CW + 3 - d, b * 2 + i),
                                in1=XC[i][:, d:], op0=ALU.mult, op1=ALU.add).then_inc(cv_r, 1)

                    def lru(b, i):
                        dve.wait_ge(i_r, at(b, 2, i + 1))
                        TT(I[:], I[:], XC[i][:], ALU.mult).then_inc(ix_r, 1)
                        dve.wait_ge(a2_r, at(b, 2, i + 1))
                        STT(out=G[:], in0=SG[:], scalar=1.0, in1=G[:], op0=ALU.add, op1=ALU.mult).then_inc(m2_r, 1)
                        dve.wait_ge(m_r, at(b, 2, i + 1))
                        dve.wait_ge(ix_r, at(b, 2, i + 1))
                        TT(I[:], I[:], G[:], ALU.mult).then_inc(lu_r, 1)
                        dve.wait_ge(lu_r, at(b, 2, i + 1))
                        dve.wait_ge(pe_g, at(b, 4, 4))
                        V_.tensor_tensor_scan(XC[i][:], R[:], I[:], 0.0, ALU.mult, ALU.add).then_inc(h_r, 1)

                    def lru_out(b, i):
                        dve.wait_ge(slg_r, at(b, 2, i + 1))
                        TT(SG[:], SG[:], prod[SLAB[SEC_LG, i] % 2][:], ALU.mult).then_inc(lg_r, 1)
                        dve.wait_ge(lg_r, at(b, 2, i + 1))
                        dve.wait_ge(h_r, at(b, 2, i + 1))
                        TT(SG[:], SG[:], XC[i][:], ALU.mult).then_inc(yl_r, 1)

                    def block_dve(b):
                        key(b, 0); diff(b, 0, 1); diff(b, 0, 2); prod_e(b, 0, 1)
                        query(b, 0)
                        diff(b, 0, 3); prod_e(b, 0, 2)
                        diff(b, 0, 4); prod_e(b, 0, 3)
                        diff(b, 0, 5); prod_e(b, 0, 4)
                        diff(b, 0, 6); prod_e(b, 0, 5)
                        states(b, 0)
                        scores(b, 0, 0); prod_e(b, 0, 6)
                        scores(b, 0, 1); prod_e(b, 0, 7)
                        scores(b, 0, 2); prod_e(b, 0, 8)
                        scores(b, 0, 3)
                        query(b, 1)
                        scores(b, 0, 4)
                        key(b, 1); diff(b, 1, 1); diff(b, 1, 2); prod_e(b, 1, 1)
                        diff(b, 1, 3); prod_e(b, 1, 2)
                        diff(b, 1, 4); prod_e(b, 1, 3)
                        norm(b, 0)
                        diff(b, 1, 5); prod_e(b, 1, 4)
                        conv(b, 0)
                        diff(b, 1, 6); prod_e(b, 1, 5)
                        states(b, 1)
                        scores(b, 1, 0); prod_e(b, 1, 6)
                        conv(b, 1)
                        scores(b, 1, 1); prod_e(b, 1, 7)
                        scores(b, 1, 2); prod_e(b, 1, 8)
                        scores(b, 1, 3)
                        head_out(b, 0)
                        scores(b, 1, 4)
                        norm(b, 1)
                        head_out(b, 1)
                        lru(b, 0)
                        lru(b, 1)
                        lru_out(b, 0)
                        lru_out(b, 1)

                    with dve.Fori(0, NB - 1) as b:
                        block_dve(b)
                    block_dve(NB - 1)

                @blk.tensor
                def _(pe):
                    start_full(pe, PER_PE)
                    M = nc.tensor.matmul

                    pe.wait_ge(c_pool, 2)
                    for t in range(NT):
                        pe.wait_ge(x_scaled, t + 1)
                        if t >= 2:
                            pe.wait_ge(u_lo, t - 1)
                        for k in range(KD):
                            last = nc.tensor.transpose(mix[t % 2][:, k * P:(k + 1) * P], xstage[t % 4][:, k * P:(k + 1) * P], ident[:])
                        last.then_inc(x_tr, 1)
                        if t == 4:
                            pe.wait_ge(p_land, 16 * 7)
                            n = NPAR * KD
                            nc.tensor.transpose(prod[1][:, 0:n], prow[0:n, 0:P], ident[0:n, 0:n]).then_inc(p_T, 1)
                    pe.wait_ge(u_lo, NT)
                    pe.wait_ge(p_par, 1)

                    frees = {SEC_F: (sf_r, 2, 1), SEC_Q: (q_r, 2, 1), SEC_V: (v_r, 2, 1), SEC_X: (cv_r, 6, 3),
                             SEC_HG: (hg_r, 2, 1), SEC_LG: (lg_r, 2, 1)}

                    def product(b, s):
                        pe.wait_ge(w_lo, at(b, NS, s + 1))
                        sec, j = SLABS[s - 2]
                        fs, per, each = frees[sec]
                        pe.wait_ge(fs, at(b, per, each * (j + 1) - (per if s < 2 else 0)))
                        hi, lo = whi[s % SLOTS], wlo[s % SLOTS]
                        n = 0
                        for half in range(2):
                            t = slice(half * HALF, (half + 1) * HALF)
                            for k in range(KD):
                                for w, u in ((hi, uhi), (hi, ulo), (lo, uhi)):
                                    last = M(prod[s % 2][:, t], w[:, k], u[:, k, t], start=(n % 24 == 0), stop=(n % 24 == 23))
                                    n += 1
                                    if n % 12 == 0:
                                        if n == 48:
                                            last.then_inc(slab, 1)
                                        for name, arg in WHEN.get(4 * s + n // 12 - 1, []):
                                            step(b, name, arg)

                    def step(b, name, h):
                        c_ = [slice(c * P, (c + 1) * P) for c in range(NC)]
                        if name == "tk":
                            pe.wait_ge(x_r, at(b, 16, 8 * h + 1))
                            pe.wait_ge(*((r_r, at(b, 2, 0)) if h == 0 else (z_r, at(b, 2, 1))))
                            for c in range(NC):
                                last = nc.tensor.transpose(mix[0][:, c_[c]], KE[:, c_[c]], ident[:])
                            last.then_inc(pe_tk, 1)
                        elif name == "tv":
                            pe.wait_ge(v_r, at(b, 2, h + 1))
                            pe.wait_ge(*((i_r, at(b, 2, 0)) if h == 0 else (ln_r, at(b, 2, 1))))
                            for c in range(NC):
                                last = nc.tensor.transpose(mix[1][:, c_[c]], V[h][:, c_[c]], ident[:])
                            last.then_inc(pe_tv, 1)
                        elif name == "u":
                            pe.wait_ge(kt_r, at(b, 2, h + 1))
                            pe.wait_ge(vt_r, at(b, 2, h + 1))
                            for c in range(NC - 1):
                                last = M(mix[0][:, c_[c]], KE[:, c_[c]], V[h][:, c_[c]], start=True, stop=True)
                            last.then_inc(pe_u, 1)
                        elif name[0] == "l":
                            i = int(name[1])
                            l = LEVELS[i]
                            pe.wait_ge(x_r, at(b, 16, 8 * h + 2 + i))
                            pe.wait_ge(*((vt_r, at(b, 2, h + 1)), (st_r, at(b, 14, 7 * (h + 1))),
                                         (sc_r, at(b, 10, 5 * h + 1)), (sc_r, at(b, 10, 5 * h + 2)))[i])
                            for c in range(NC):
                                second = X4[i][:, c_[c]].rearrange("p (i t) -> p i t", t=2 * l)[:, :, l:]
                                last = M(mix[(1, 0, 1, 0)[i]][:, c * 64:(c + 1) * 64], X4[i][:, c_[c]], second,
                                         start=True, stop=True)
                            last.then_inc(pe_l, 1)
                        elif name == "dg":
                            pe.wait_ge(x_r, at(b, 16, 8 * h + 7))
                            pe.wait_ge(sc_r, at(b, 10, 5 * h + 3))
                            for c in range(NC):
                                last = M(mix[1][:, c_[c]], X4[1][:, c_[c]], X4[0][:, c_[c]], start=True, stop=True)
                            last.then_inc(pe_dg, 1)
                        elif name == "o":
                            pe.wait_ge(x_r, at(b, 16, 8 * h + 8))
                            pe.wait_ge(sc_r, at(b, 10, 5 * h + 5))
                            pe.wait_ge(st_r, at(b, 14, 7 * (h + 1)))
                            for c in range(NC):
                                last = M(mix[0][:, c_[c]], V[h][:, c_[c]], S[:, c], start=True, stop=(c == 0))
                                if c:
                                    last = M(mix[0][:, c_[c]], ST[:, c], QE[:, c_[c]], start=False, stop=True)
                            last.then_inc(pe_o, 1)
                        elif name == "ms":
                            pe.wait_ge(o2_r, at(b, 2, h + 1))
                            for half in range(2):
                                t = slice(half * HALF, (half + 1) * HALF)
                                last = M(mix[1][:, t], ones[:], G[:, t], start=True, stop=True)
                            last.then_inc(pe_ms, 1)
                        elif name == "g":
                            i, gate_ = h // 2, h % 2
                            pe.wait_ge(cv_r, at(b, 6, 6))
                            for g in range(2):
                                pe.wait_ge(g_land[g], b * 16 + 16)
                            pe.wait_ge(*((z_r, at(b, 2, 2)), (ln_r, at(b, 2, 2)), (r_r, at(b, 2, 1)), (i_r, at(b, 2, 1)))[h])
                            for half in range(2):
                                t = slice(half * HALF, (half + 1) * HALF)
                                for k in range(2):
                                    last = M(mix[h % 2][:, t], gw[:, gate_, k, i * P:(i + 1) * P], XC[k][:, t],
                                             start=(k == 0), stop=(k == 1))
                            last.then_inc(pe_g, 1)

                    with pe.Fori(0, NB - 1) as b:
                        for s in range(NS):
                            product(b, s)
                    for s in range(NS):
                        product(NB - 1, s)

        GT = 2 * P
        NG = T // GT
        order = [m for m0, m1 in PIECES for m in range(m0, m1)]
        NPC = len(PIECES)
        wr_land = [sem(f"wr_land{i}") for i in range(2)]
        yr_land = [sem(f"yr_land{i}") for i in range(NPC)]
        xr_land = [sem(f"xr_land{i}") for i in range(2)]
        po_st = [sem(f"po_st{i}") for i in range(2)]
        (pw2_land, wo_hi, wo_lo, yh_r, yl2_r, pe_pc, pe_grp, sq2_r, ln2_r, rs2_r, o1_r, o2o_r) = [sem(n) for n in (
            "pw2_land wo_hi wo_lo yh_r yl2_r pe_pc pe_grp sq2_r ln2_r rs2_r o1_r o2o_r").split()]
        with ExitStack() as octx:
            def ob(name, shape, dt=F32):
                return octx.enter_context(nc.sbuf_tensor(name, shape, dt))

            WH, WL = ob("WH", [P, MT, D], F32R), ob("WL", [P, MT, D], F32R)
            YH, YL = ob("YH", [P, MT, GT], F32R), ob("YL", [P, MT, GT], F32R)
            YR = ob("YR", [P, MT, GT])
            WR = [ob(f"WR{i}", [P, D]) for i in range(2)]
            pwo = ob("pwo", [P, D])
            XR = [ob(f"XR{i}", [P, D]) for i in range(2)]
            OT = [ob(f"OT{i}", [P, D]) for i in range(2)]

            x_v = x[0].rearrange("(t p) d -> t p d", p=P)
            o_v = out[0].rearrange("(t p) d -> t p d", p=P)
            wo_v = w_out[0].rearrange("(m p) d -> m p d", p=P)
            y_g = y_scr.rearrange("m p (g t) -> p g m t", t=GT)

            with nc.Block() as blk:
                @blk.sync
                def _(sp):
                    for eng_, per in ((sp, {yh_r: NPC, yl2_r: NPC, pe_pc: NPC, pe_grp: 1, o1_r: 2, o2o_r: 2, sq2_r: 2,
                                            ln2_r: 2, rs2_r: 2, po_st[0]: 16, po_st[1]: 16}),):
                        start_full(eng_, per)
                    sp.dma_start(pwo[:], post_norm_w.to_broadcast([P, D])).then_inc(pw2_land, 16)

                    def load_w(i):
                        if i >= 2:
                            sp.wait_ge(wo_lo, i - 1)
                        sp.dma_start(WR[i % 2][:], wo_v[order[i]]).then_inc(wr_land[i % 2], 16)

                    def load_y(g, p):
                        m0, m1 = PIECES[p]
                        sp.dma_start(YR[:, m0:m1, :], y_g[:, g, m0:m1, :]).then_inc(yr_land[p], 16)

                    load_w(0); load_y(0, 0); load_w(1); load_y(0, 1)
                    for i in range(2, MT):
                        load_w(i)
                        if i == 3:
                            load_y(0, 2); load_y(0, 3)
                            for j in range(2):
                                sp.dma_start(XR[j][:], x_v[j]).then_inc(xr_land[j], 16)
                    for g in range(NG):
                        if g + 1 < NG:
                            for p in range(NPC):
                                sp.wait_ge(yl2_r, at(g, NPC, p + 1))
                                load_y(g + 1, p)
                        for j in range(2):
                            sp.wait_ge(o2o_r, at(g, 2, j + 1))
                            sp.dma_start(o_v[2 * g + j], OT[j][:]).then_inc(po_st[j], 16)
                            if g + 1 < NG:
                                sp.dma_start(XR[j][:], x_v[2 * g + 2 + j]).then_inc(xr_land[j], 16)
                    for j in range(2):
                        sp.wait_ge(po_st[j], at(NG, 16, 0))

                @blk.scalar
                def _(act):
                    A = nc.scalar.activation

                    def y_high(g, p):
                        m0, m1 = PIECES[p]
                        act.wait_ge(yr_land[p], 16 * (g + 1))
                        act.wait_ge(pe_pc, at(g, NPC, p + 1 - NPC))
                        A(YH[:, m0:m1], YR[:, m0:m1], ACT.Copy).then_inc(yh_r, 1)

                    def w_high(i):
                        act.wait_ge(wr_land[i % 2], 16 * (i // 2 + 1))
                        A(WH[:, order[i]], WR[i % 2][:], ACT.Copy).then_inc(wo_hi, 1)

                    def rstd(g, j):
                        acc = (prod, mix)[g % 2][j]
                        c = 2 * g + j
                        if j == 0:
                            act.wait_ge(pe_grp, at(g, 1, 1))
                        else:
                            act.wait_ge(pe_pc, at(g, NPC, NPC))
                        act.wait_ge(po_st[j], at(g, 16, 0))
                        A(OT[j][:], acc[:], ACT.Square, accum_out=ssq[:, c:c + 1]).then_inc(sq2_r, 1)
                        act.wait_ge(sq2_r, at(g, 2, j + 1))
                        A(rst[:, c:c + 1], ssq[:, c:c + 1], ACT.Ln, scale=1.0 / D, bias=eps_c[:]).then_inc(ln2_r, 1)
                        act.wait_ge(ln2_r, at(g, 2, j + 1))
                        A(rst[:, c:c + 1], rst[:, c:c + 1], ACT.Exp, scale=-0.5).then_inc(rs2_r, 1)

                    w_high(0); y_high(0, 0)
                    for i in range(1, MT):
                        w_high(i)
                        if i in (2, 4, 6):
                            y_high(0, i // 2)
                    for g in range(NG):
                        if g + 1 < NG:
                            y_high(g + 1, 0)
                            y_high(g + 1, 1)
                            y_high(g + 1, 2)
                        rstd(g, 0)
                        rstd(g, 1)
                        if g + 1 < NG:
                            y_high(g + 1, 3)

                @blk.vector
                def _(dve):
                    TT = nc.vector.tensor_tensor

                    def y_low(g, p):
                        m0, m1 = PIECES[p]
                        dve.wait_ge(yh_r, at(g, NPC, p + 1))
                        TT(YL[:, m0:m1], YR[:, m0:m1], YH[:, m0:m1], ALU.subtract).then_inc(yl2_r, 1)

                    def w_low(i):
                        dve.wait_ge(wo_hi, i + 1)
                        TT(WL[:, order[i]], WR[i % 2][:], WH[:, order[i]], ALU.subtract).then_inc(wo_lo, 1)

                    def finish(g, j):
                        acc = (prod, mix)[g % 2][j]
                        c = 2 * g + j
                        dve.wait_ge(rs2_r, at(g, 2, j + 1))
                        dve.wait_ge(pw2_land, 16)
                        nc.vector.scalar_tensor_tensor(out=OT[j][:], in0=acc[:], scalar=rst[:, c:c + 1], in1=pwo[:],
                                                       op0=ALU.mult, op1=ALU.mult).then_inc(o1_r, 1)
                        dve.wait_ge(o1_r, at(g, 2, j + 1))
                        dve.wait_ge(xr_land[j], 16 * (g + 1))
                        TT(OT[j][:], OT[j][:], XR[j][:], ALU.add).then_inc(o2o_r, 1)

                    w_low(0); y_low(0, 0)
                    for i in range(1, MT):
                        w_low(i)
                        if i in (2, 4, 6):
                            y_low(0, i // 2)
                    for g in range(NG):
                        if g + 1 < NG:
                            y_low(g + 1, 0)
                            y_low(g + 1, 1)
                            y_low(g + 1, 2)
                        finish(g, 0)
                        finish(g, 1)
                        if g + 1 < NG:
                            y_low(g + 1, 3)

                @blk.tensor
                def _(pe):
                    M = nc.tensor.matmul
                    for g in range(NG):
                        acc = (prod, mix)[g % 2]
                        i = 0
                        if g >= 2:
                            pe.wait_ge(o1_r, at(g, 2, -2))
                        for p, (m0, m1) in enumerate(PIECES):
                            pe.wait_ge(yl2_r, at(g, NPC, p + 1))
                            for m in range(m0, m1):
                                if g == 0:
                                    pe.wait_ge(wo_lo, i + 1)
                                for j in range(2):
                                    tok = slice(j * P, (j + 1) * P)
                                    n = 0
                                    for y, w in ((YH, WH), (YH, WL), (YL, WH)):
                                        for half in range(2):
                                            d = slice(half * HALF, (half + 1) * HALF)
                                            last = M(acc[j][:, d], y[:, m, tok], w[:, m, d], start=(i == 0 and n < 2),
                                                     stop=(i == MT - 1 and n >= 4))
                                            n += 1
                                    if i == MT - 1 and j == 0:
                                        last.then_inc(pe_grp, 1)
                                i += 1
                            last.then_inc(pe_pc, 1)


INS = ["x", "pre_norm_w", "w_in", "conv_w", "conv_b", "lru_w_a", "lru_b_a", "lru_w_x", "lru_b_x", "lru_lambda",
       "hgrn_lb_logits", "hgrn_gnorm_w", "w_out", "post_norm_w"]


def kernel(**inputs):
    import numpy as np
    import concourse.bacc as bacc
    from concourse.bass_utils import run_bass_kernel_spmd

    nc = bacc.Bacc("TRN2", target_bir_lowering=False, num_devices=1)
    arrays, args = {}, []
    for name in INS:
        a = np.ascontiguousarray(inputs[name])
        arrays[f"in_{name}"] = a
        args.append(nc.dram_tensor(f"in_{name}", a.shape, mybir.dt.from_np(a.dtype), kind="ExternalInput").ap())
    _, seq, width = inputs["x"].shape
    out = nc.dram_tensor("out_h", (1, seq, width), F32, kind="ExternalOutput").ap()
    scratch = nc.dram_tensor("mixed", (inputs["w_out"].shape[1] // P, P, seq), F32, kind="Internal").ap()
    build(nc, *args, out, scratch)
    r = run_bass_kernel_spmd(nc, [arrays], core_ids=[0])
    return r.results[0]["out_h"]
```

```python
from contextlib import ExitStack

import concourse.bass as bass
from concourse import mybir

F32 = mybir.dt.float32
F32R = mybir.dt.float32r
I8 = mybir.dt.int8
ALU = mybir.AluOpType
ACT = mybir.ActivationFunctionType

P = 128
EPS = 1e-6
F_FLOOR = 1e-9
M_FLOOR = 2.0 ** -60
LRU_C = 8.0
LEVELS = (64, 32, 16, 8)
SUB = 8
HALF = 512
SLOTS = 3

CW, CB, BA, BX, LAM, LB0, LB1, GN = 0, 4, 5, 6, 7, 8, 9, 10
NPAR = 11
LBC, OML, NOML, C8, NC8, TMP = 0, 1, 2, 3, 4, 5
NDER = 13

SEC_X, SEC_LG, SEC_Q, SEC_F, SEC_V, SEC_HG = range(6)
SLABS = [(SEC_X, 0), (SEC_X, 1), (SEC_F, 0), (SEC_Q, 0), (SEC_V, 0), (SEC_F, 1), (SEC_Q, 1), (SEC_V, 1),
         (SEC_LG, 0), (SEC_LG, 1), (SEC_HG, 0), (SEC_HG, 1)]
NS = len(SLABS)
SLAB = {sj: s for s, sj in enumerate(SLABS)}

WHEN = {}
for _n, _q in enumerate((11, 11, 11, 11)):
    WHEN.setdefault(_q, []).append(("g", _n))
for _h, _qs in enumerate([(17, 21, 22, 23, 24, 25, 26, 27, 29, 32), (35, 36, 37, 38, 39, 40, 41, 42, 44, 46)]):
    for _s, _q in zip(["tk", "tv", "u", "l0", "l1", "l2", "l3", "dg", "o", "ms"], _qs):
        WHEN.setdefault(_q, []).append((_s, _h))

PIECES = [(0, 6), (8, 14), (6, 8), (14, 16)]


def at(b, per, n):
    return (b + 1) * per + n


def build(nc, x, pre_norm_w, w_in, conv_w, conv_b, lru_w_a, lru_b_a, lru_w_x, lru_b_x, lru_lambda,
          hgrn_lb_logits, hgrn_gnorm_w, w_out, post_norm_w, out, y_scr):
    T, D = x.shape[1], x.shape[2]
    NT, KD, MT = T // P, D // P, w_out.shape[1] // P
    NB, NC = KD // 2, T // P
    assert T == 1024 and D == 1024 and MT == 2 * KD

    ctx = ExitStack()
    with ctx:
        def sem(name):
            return ctx.enter_context(nc.semaphore(name))

        def sb(name, shape, dt=F32, c=ctx):
            return c.enter_context(nc.sbuf_tensor(name, shape, dt))

        ident = sb("ident", [P, P])
        ones = sb("ones", [P, P], F32R)
        maskl = [sb(f"mask{l}", [P, 1, P // (2 * l), l], I8) for l in LEVELS]
        maskd = sb("maskd", [P, 1, P], I8)
        keep = sb("keep", [P, T], I8)
        eps_c = sb("eps_c", [P, 1])
        mfl_c = sb("mfl_c", [P, 1])
        par = sb("par", [P, NPAR, KD])
        der = sb("der", [P, NDER, KD])
        dec = sb("dec", [P, NC])
        ssq = sb("ssq", [P, NT])
        rst = sb("rst", [P, NT])
        gate = sb("gate", [1, 1])

        prod = [ctx.enter_context(nc.psum_tensor(f"prod{i}", [P, T], F32)) for i in range(2)]
        mix = [ctx.enter_context(nc.psum_tensor(f"mix{i}", [P, T], F32)) for i in range(2)]

        c_pool, c_const, p_land, p_T, p_par, p_dve, p_act, pw_land = [sem(n) for n in (
            "c_pool c_const p_land p_T p_par p_dve p_act pw_land").split()]
        x_land = [sem(f"x_land{i}") for i in range(4)]
        x_ssq, x_ln, x_rst, x_scaled, x_tr, u_hi, u_lo = [sem(n) for n in (
            "x_ssq x_ln x_rst x_scaled x_tr u_hi u_lo").split()]
        w_land = [sem(f"w_land{i}") for i in range(2)]
        wx_land = [sem(f"wx_land{i}") for i in range(2)]
        g_land = [sem(f"g_land{i}") for i in range(2)]
        w_hi, w_lo, slab = sem("w_hi"), sem("w_lo"), sem("slab")
        sf_r, sq_r, v_r, lf_r, k_r, b_r, q_r = [sem(n) for n in "sf_r sq_r v_r lf_r k_r b_r q_r".split()]
        d_r, e_r, x_r, dec_r = [sem(n) for n in "d_r e_r x_r dec_r".split()]
        pe_tk, pe_tv, pe_u, pe_l, pe_dg, pe_o, pe_ms, pe_g = [sem(n) for n in (
            "pe_tk pe_tv pe_u pe_l pe_dg pe_o pe_ms pe_g").split()]
        kt_r, vt_r, st_r, sc_r, o2_r, ln_r, rs_r, z_r = [sem(n) for n in "kt_r vt_r st_r sc_r o2_r ln_r rs_r z_r".split()]
        shg_r, hg_r, y_r = [sem(n) for n in "shg_r hg_r y_r".split()]
        gwh_r, gwl_r, xh_r, xl_r, o2h_r, o2l_r = [sem(n) for n in "gwh_r gwl_r xh_r xl_r o2h_r o2l_r".split()]
        xt_r, cv_r, r_r, i_r, th_r, a_r, a2_r, m2_r, ml_r, m_r = [sem(n) for n in (
            "xt_r cv_r r_r i_r th_r a_r a2_r m2_r ml_r m_r").split()]
        ix_r, lu_r, h_r, slg_r, lg_r, yl_r = [sem(n) for n in "ix_r lu_r h_r slg_r lg_r yl_r".split()]
        yh_st = [sem(f"yh_st{i}") for i in range(2)]
        yl_st = sem("yl_st")

        PER_PE = {slab: NS, pe_tk: 2, pe_tv: 2, pe_u: 2, pe_l: 8, pe_dg: 2, pe_o: 2, pe_ms: 2, pe_g: 4}
        PER_ACT = {w_hi: NS, sf_r: 2, sq_r: 2, v_r: 2, lf_r: 2, e_r: 16, dec_r: 2, kt_r: 2, vt_r: 2, o2_r: 2, o2h_r: 2,
                   gwh_r: 1, xh_r: 2, ln_r: 2, rs_r: 2,
                   shg_r: 2, xt_r: 2, r_r: 2, i_r: 2, th_r: 2, a_r: 2, a2_r: 2, ml_r: 2, m_r: 2, slg_r: 2, yl_st: 32}
        PER_DVE = {gwl_r: 1, xl_r: 2, o2l_r: 2, k_r: 2, b_r: 2, q_r: 2, d_r: 12, x_r: 16, st_r: 14, sc_r: 10, z_r: 2, hg_r: 2, y_r: 2,
                   cv_r: 6, m2_r: 2, ix_r: 2, lu_r: 2, h_r: 2, lg_r: 2, yl_r: 2}
        PER_POOL = {w_lo: NS}
        PER_SP = {yh_st[0]: 16, yh_st[1]: 16}

        def start_full(eng, per):
            for s, n in per.items():
                eng.sem_inc(s, n)

        with ExitStack() as mctx:
            def mb(name, shape, dt=F32):
                return mctx.enter_context(nc.sbuf_tensor(name, shape, dt))

            uhi = mb("uhi", [P, KD, T], F32R)
            ulo = mb("ulo", [P, KD, T], F32R)
            whi = [mb(f"whi{i}", [P, KD, P], F32R) for i in range(SLOTS)]
            wlo = [mb(f"wlo{i}", [P, KD, P], F32R) for i in range(SLOTS)]
            wraw = [mb(f"wraw{i}", [P, KD, P]) for i in range(2)]
            gw = mb("gw", [P, 2, 2, 2 * P])
            with ExitStack() as actx:
                xch = [sb(f"xch{i}", [P, T], F32R, actx) for i in range(2)]
                xcl = [sb(f"xcl{i}", [P, T], F32R, actx) for i in range(2)]
                gwh, gwl = [sb(n, [P, 2, 2, 2 * P], F32R, actx) for n in ("gwh", "gwl")]
                o2h, o2l = [sb(n, [P, T], F32R, actx) for n in ("o2h", "o2l")]
            X4 = [mb(f"X{i}", [P, T]) for i in range(4)]
            QE = mb("QE", [P, T])
            ST = mb("ST", [P, NC, P])
            R, I = mb("R", [P, T]), mb("I", [P, T])
            K = [mb(f"K{h}", [P, T]) for h in range(2)]
            Q = [mb(f"Q{h}", [P, T]) for h in range(2)]
            V = [mb(f"V{h}", [P, T]) for h in range(2)]
            XC = [mb(f"XC{h}", [P, T]) for h in range(2)]
            Bs = mb("Bs", [P, T])
            S = mb("S", [P, NC, P])
            Dt = [mb(f"D{i}", [P, T]) for i in range(2)]
            Et = [mb(f"E{i}", [P, T]) for i in range(2)]
            KE = mb("KE", [P, T])
            G, SG = mb("G", [P, T]), mb("SG", [P, T])
            Rg, Ig, Gg = (R, K[1]), (I, Q[1]), (G, V[1])
            xstage = [R, I, Bs, QE]
            pwb, prow = XC[0], XC[1]

            x_v = x[0].rearrange("(t p) d -> t p d", p=P)
            w_v = w_in[0].rearrange("(k p) (s j c) -> p k s j c", p=P, s=6, c=P)
            ga_v = lru_w_a[0].rearrange("n (k p) c -> p n k c", p=P)
            gx_v = lru_w_x[0].rearrange("n (k p) c -> p n k c", p=P)
            y_v = y_scr.rearrange("m p t -> p m t")

            def col(table, row, j):
                return table[:, row, bass.ds(j, 1)]

            def chunks(t_, w=P):
                return t_[:].rearrange("p (c t) -> p c t", t=w)

            def known(eng, v):
                return v if isinstance(v, int) else eng.snap(v)

            with nc.Block() as blk:
                @blk.sync
                def _(sp):
                    start_full(sp, PER_SP)
                    rows = [(conv_w[0].rearrange("k (j p) -> (k j) p", p=P), 4 * KD),
                            (conv_b.rearrange("a (j p) -> (a j) p", p=P), KD),
                            (lru_b_a[0].rearrange("n (j p) -> (n j) p", p=P), KD),
                            (lru_b_x[0].rearrange("n (j p) -> (n j) p", p=P), KD),
                            (lru_lambda.rearrange("a (j p) -> (a j) p", p=P), KD),
                            (hgrn_lb_logits.rearrange("a (j p) -> (a j) p", p=P), 2 * KD),
                            (hgrn_gnorm_w.rearrange("a (j p) -> (a j) p", p=P), KD)]
                    sp.dma_start(xstage[0][:], x_v[0]).then_inc(x_land[0], 16)
                    sp.dma_start(pwb[:], pre_norm_w.to_broadcast([P, D])).then_inc(pw_land, 16)
                    sp.dma_start(xstage[1][:], x_v[1]).then_inc(x_land[1], 16)
                    n = 0
                    for src, cnt in rows:
                        sp.dma_start(prow[n:n + cnt, 0:P], src).then_inc(p_land, 16)
                        n += cnt
                    for t in range(2, 4):
                        sp.dma_start(xstage[t][:], x_v[t]).then_inc(x_land[t], 16)
                    for g, src in enumerate((ga_v, gx_v)):
                        sp.dma_start(gw[:, g], src[:, 0]).then_inc(g_land[g], 16)
                    for s in range(2):
                        sec, j = SLABS[s]
                        sp.dma_start(wraw[s][:], w_v[:, :, sec, j, :]).then_inc(w_land[s], 16)
                    for t in range(4, NT):
                        sp.wait_ge(x_tr, t - 3)
                        sp.dma_start(xstage[t % 4][:], x_v[t]).then_inc(x_land[t % 4], 16)

                    def load_block(b, last):
                        for k in range(2, NS if last else NS + 2):
                            sec, j = SLABS[k % NS]
                            if sec == SEC_X:
                                continue
                            jj = b * 2 + j + (2 if k >= NS else 0)
                            need = known(sp, at(b, NS, k - 1))
                            sp.wait_ge(w_lo, need)
                            sp.dma_start(wraw[k % 2][:], w_v[:, :, sec, bass.ds(jj, 1), :].rearrange("p k j c -> p k (j c)")
                                         ).then_inc(w_land[k % 2], 16)
                            if k in (8, 9) and not last:
                                src = (ga_v, gx_v)[k - 8]
                                need = known(sp, at(b, 1, 1))
                                sp.wait_ge(gwl_r, need)
                                sp.dma_start(gw[:, k - 8], src[:, bass.ds(b + 1, 1)].rearrange("p n k c -> p (n k) c")
                                             ).then_inc(g_land[k - 8], 16)
                        for h in range(2):
                            m = known(sp, b * 2 + h + KD)
                            need = known(sp, at(b, 2, h + 1))
                            sp.wait_ge(y_r, need)
                            sp.dma_start(y_v[:, bass.ds(m, 1), :].rearrange("p m t -> p (m t)"), V[h][:]).then_inc(yh_st[h], 16)

                    with sp.Fori(0, NB - 1) as b:
                        load_block(b, False)
                    load_block(NB - 1, True)
                    for h in range(2):
                        sp.wait_ge(yh_st[h], at(NB, 16, 0))

                @blk.gpsimd
                def _(pool):
                    start_full(pool, PER_POOL)
                    n = [0]

                    def step(ins):
                        n[0] += 1
                        ins.then_inc(c_pool, 1)
                        pool.wait_ge(c_pool, n[0])

                    step(pool.memset(ident[:], 0.0))
                    step(pool.affine_select(out=ident[:], in_=ident[:], compare_op=ALU.not_equal, fill=1.0, base=0,
                                            pattern=[[-1, P]], channel_multiplier=1))
                    step(pool.memset(eps_c[:], EPS))
                    step(pool.memset(SG[:, 0:P], 1.0 / P))
                    pool.tensor_copy(ones[:], SG[:, 0:P])
                    pool.memset(mfl_c[:], M_FLOOR)
                    pool.memset(S[:], 0.0)
                    step(pool.memset(keep[:], 1))
                    step(pool.memset(keep[:].rearrange("p (c t) -> p c t", t=P)[:, :, 0:1], 0))
                    for l, m in zip(LEVELS, maskl):
                        mm = m[:, 0]
                        step(pool.memset(m[:], 1))
                        step(pool.affine_select(out=mm, in_=mm, compare_op=ALU.is_ge, fill=0, base=0,
                                                pattern=[[-2 * l, P // (2 * l)], [0, l]], channel_multiplier=1))
                        step(pool.affine_select(out=mm, in_=mm, compare_op=ALU.is_ge, fill=0, base=l - 1,
                                                pattern=[[2 * l, P // (2 * l)], [0, l]], channel_multiplier=-1))
                    md = maskd[:, 0].rearrange("p (i t) -> p i t", t=SUB)
                    step(pool.memset(maskd[:], 1))
                    step(pool.affine_select(out=md, in_=md, compare_op=ALU.is_ge, fill=0, base=0,
                                            pattern=[[-SUB, P // SUB], [0, SUB]], channel_multiplier=1))
                    pool.affine_select(out=md, in_=md, compare_op=ALU.is_ge, fill=0, base=0,
                                       pattern=[[SUB, P // SUB], [1, SUB]], channel_multiplier=-1).then_inc(c_const, 1)

                    def low_parts(b, ks, last=False):
                        for k in ks:
                            pool.wait_ge(w_hi, at(b, NS, k + 1))
                            pool.tensor_tensor(wlo[k % SLOTS][:], wraw[k % 2][:], whi[k % SLOTS][:],
                                               ALU.subtract).then_inc(w_lo, 1)
                            sec, j = SLABS[(k + 2) % NS]
                            if sec == SEC_X and not last:
                                pool.wait_ge(w_lo, at(b, NS, k + 1))
                                pool.dma_start(wraw[k % 2][:], w_v[:, :, sec, bass.ds(b * 2 + j + 2, 1), :].rearrange(
                                    "p k j c -> p k (j c)")).then_inc(wx_land[j], 16)

                    low_parts(0, range(3))
                    with pool.Fori(0, NB - 1) as b:
                        low_parts(b, range(3, NS + 3))
                    low_parts(NB - 1, range(3, NS), True)

                @blk.scalar
                def _(act):
                    start_full(act, PER_ACT)
                    A = nc.scalar.activation

                    def high_part(b, k):
                        sec, j = SLABS[k % NS]
                        if sec == SEC_X and isinstance(b, int) and b == 0 and k < NS:
                            act.wait_ge(w_land[k % 2], 16)
                        elif sec == SEC_X:
                            act.wait_ge(wx_land[j], b * 16 + 16)
                        else:
                            before = sum(s % 2 == k % 2 and SLABS[s][0] != SEC_X for s in range(k % NS))
                            act.wait_ge(w_land[k % 2], (b + k // NS) * 80 + (before + 2) * 16)
                        act.wait_ge(slab, at(b, NS, k - 2))
                        A(whi[k % SLOTS][:], wraw[k % 2][:], ACT.Copy).then_inc(w_hi, 1)

                    loaded = [None]

                    def table(name):
                        if loaded[0] != name:
                            loaded[0] = name
                            nc.scalar.preload_act_table_set(name)

                    LOG_EXP, SIGMOID = "natural_log_exp_and_others", "sigmoid_and_others"
                    table(LOG_EXP)
                    for t in range(NT):
                        act.wait_ge(x_land[t % 4], 16 * (t // 4 + 1))
                        if t >= 1:
                            act.wait_ge(x_ssq, t)
                        A(Et[0][:], xstage[t % 4][:], ACT.Square, accum_out=ssq[:, t:t + 1]).then_inc(x_ssq, 1)
                        act.wait_ge(x_ssq, t + 1)
                        act.wait_ge(c_pool, 3)
                        A(rst[:, t:t + 1], ssq[:, t:t + 1], ACT.Ln, scale=1.0 / D, bias=eps_c[:]).then_inc(x_ln, 1)
                        act.wait_ge(x_ln, t + 1)
                        A(rst[:, t:t + 1], rst[:, t:t + 1], ACT.Exp, scale=-0.5).then_inc(x_rst, 1)
                        if 2 <= t < 4:
                            high_part(0, t - 2)
                        if t >= 1:
                            act.wait_ge(x_tr, t)
                            A(uhi[:, :, (t - 1) * P:t * P], chunks(mix[(t - 1) % 2]), ACT.Copy).then_inc(u_hi, 1)
                    act.wait_ge(x_tr, NT)
                    A(uhi[:, :, T - P:], chunks(mix[(NT - 1) % 2]), ACT.Copy).then_inc(u_hi, 1)
                    act.wait_ge(p_dve, 4)
                    A(der[:, TMP + 0], der[:, TMP + 0], ACT.Exp).then_inc(p_act, 1)
                    A(der[:, TMP + 1], der[:, TMP + 1], ACT.Exp).then_inc(p_act, 1)
                    A(der[:, TMP + 2], der[:, TMP + 2], ACT.Exp, scale=-1.0).then_inc(p_act, 1)
                    high_part(0, 2)

                    def forget_gate(b, h):
                        s = SLAB[SEC_F, h]
                        act.wait_ge(slab, at(b, NS, s + 1))
                        act.wait_ge(x_r, at(b, 16, 8 * h - 8))
                        if h == 1:
                            act.wait_ge(h_r, at(b, 2, 2))
                        A(K[h][:], prod[s % 2][:], ACT.Sigmoid).then_inc(sf_r, 1)

                    def log_f(b, h):
                        act.wait_ge(sf_r, at(b, 2, h + 1))
                        act.wait_ge(e_r, at(b, 16, 8 * h))
                        A(Bs[:], K[h][:], ACT.Ln, scale=col(der, OML, b * 2 + h),
                          bias=col(der, LBC, b * 2 + h)).then_inc(lf_r, 1)

                    def exps(b, h, n):
                        e = Et[(n - 1) % 2]
                        if n == 6:
                            act.wait_ge(b_r, at(b, 2, h + 1))
                        else:
                            act.wait_ge(d_r, at(b, 12, 6 * h + min(n, 6)))
                        act.wait_ge(x_r, at(b, 16, 8 * h + n - 2))
                        if 2 <= n <= 5:
                            l = LEVELS[n - 2]
                            dv, ev = chunks(Dt[(n - 1) % 2], 2 * l), chunks(e, 2 * l)
                            A(ev[:, :, 0:l], dv[:, :, 0:l], ACT.Exp, scale=-1.0)
                            A(ev[:, :, l:], dv[:, :, l:], ACT.Exp).then_inc(e_r, 1)
                        elif n == 6:
                            A(e[:], Bs[:], ACT.Exp).then_inc(e_r, 1)
                        else:
                            A(e[:], Dt[(min(n, 6) - 1) % 2][:], ACT.Exp, scale=1.0 if n == 7 else -1.0).then_inc(e_r, 1)

                    def chunk_decay(b, h):
                        act.wait_ge(b_r, at(b, 2, h + 1))
                        act.wait_ge(st_r, at(b, 14, 7 * h))
                        A(dec[:], chunks(Bs)[:, :, P - 1], ACT.Exp).then_inc(dec_r, 1)

                    def query_gate(b, h):
                        s = SLAB[SEC_Q, h]
                        act.wait_ge(slab, at(b, NS, s + 1))
                        act.wait_ge(y_r, at(b, 2, h - 1))
                        A(Q[h][:], prod[s % 2][:], ACT.Sigmoid).then_inc(sq_r, 1)

                    def values(b, h):
                        s = SLAB[SEC_V, h]
                        act.wait_ge(slab, at(b, NS, s + 1))
                        act.wait_ge(yh_st[h], at(b, 16, 0))
                        A(V[h][:], prod[s % 2][:], ACT.Copy).then_inc(v_r, 1)

                    def keys_by_token(b, h):
                        act.wait_ge(pe_tk, at(b, 2, h + 1))
                        A(KE[:], mix[0][:], ACT.Copy).then_inc(kt_r, 1)

                    def values_by_token(b, h):
                        act.wait_ge(pe_tv, at(b, 2, h + 1))
                        A(V[h][:], mix[1][:], ACT.Copy).then_inc(vt_r, 1)

                    def gate_weights_high(b):
                        for g in range(2):
                            act.wait_ge(g_land[g], b * 16 + 16)
                        act.wait_ge(pe_o, at(b, 2, 0))
                        A(gwh[:], gw[:], ACT.Copy).then_inc(gwh_r, 1)

                    def conv_high(b, i):
                        act.wait_ge(cv_r, at(b, 6, 3 * i + 3))
                        act.wait_ge(pe_dg, at(b, 2, 0))
                        A(xch[i][:], XC[i][:], ACT.Copy).then_inc(xh_r, 1)

                    def square_out(b, h):
                        act.wait_ge(pe_o, at(b, 2, h + 1))
                        act.wait_ge(z_r, at(b, 2, h))
                        act.wait_ge(lu_r, at(b, 2, 2))
                        A(G[:], mix[0][:], ACT.Square).then_inc(o2_r, 1)
                        act.wait_ge(o2_r, at(b, 2, h + 1))
                        act.wait_ge(h_r, at(b, 2, 2))
                        act.wait_ge(pe_ms, at(b, 2, h))
                        A(o2h[:], G[:], ACT.Copy).then_inc(o2h_r, 1)

                    def head_rstd(b, h):
                        act.wait_ge(pe_ms, at(b, 2, h + 1))
                        A(G[:], mix[1][:], ACT.Ln, bias=eps_c[:]).then_inc(ln_r, 1)
                        act.wait_ge(ln_r, at(b, 2, h + 1))
                        A(G[:], G[:], ACT.Exp, scale=-0.5).then_inc(rs_r, 1)

                    def head_gate(b, h):
                        s = SLAB[SEC_HG, h]
                        act.wait_ge(slab, at(b, NS, s + 1))
                        act.wait_ge(pe_o, at(b, 2, h + 1))
                        A(V[h][:], prod[s % 2][:], ACT.Sigmoid).then_inc(shg_r, 1)

                    def first_tap(b, i):
                        s = SLAB[SEC_X, i]
                        act.wait_ge(slab, at(b, NS, s + 1))
                        act.wait_ge(yl_r, at(b, 2, i - 1))
                        act.wait_ge(p_dve, 1)
                        A(XC[i][:], prod[s % 2][:], ACT.Identity, scale=col(par, CW + 3, b * 2 + i),
                          bias=col(par, CB, b * 2 + i)).then_inc(xt_r, 1)

                    def lru_gates(b, i):
                        act.wait_ge(pe_g, at(b, 4, 2 * i + 1))
                        if i == 1:
                            act.wait_ge(x_r, at(b, 16, 0))
                            act.wait_ge(y_r, at(b, 2, 0))
                            act.wait_ge(yh_st[1], at(b, 16, 0))
                        A(Rg[i][:], mix[0][:], ACT.Sigmoid, bias=col(par, BA, b * 2 + i)).then_inc(r_r, 1)
                        act.wait_ge(pe_g, at(b, 4, 2 * i + 2))
                        A(Ig[i][:], mix[1][:], ACT.Sigmoid, bias=col(par, BX, b * 2 + i)).then_inc(i_r, 1)
                        act.wait_ge(r_r, at(b, 2, i + 1))
                        act.wait_ge(z_r, at(b, 2, 0))
                        act.wait_ge(p_par, 1)
                        A(Gg[i][:], Rg[i][:], ACT.Tanh, scale=col(der, C8, b * 2 + i)).then_inc(th_r, 1)

                    def lru_decay(b, i):
                        act.wait_ge(th_r, at(b, 2, i + 1))
                        A(Rg[i][:], Rg[i][:], ACT.Exp, scale=col(der, NC8, b * 2 + i)).then_inc(a_r, 1)
                        act.wait_ge(a_r, at(b, 2, i + 1))
                        if i == 0:
                            act.wait_ge(yl_st, at(b, 32, 0))
                        else:
                            act.wait_ge(m2_r, at(b, 2, 1))
                        A(SG[:], Rg[i][:], ACT.Square).then_inc(a2_r, 1)

                    def lru_input(b, i):
                        act.wait_ge(m2_r, at(b, 2, i + 1))
                        A(Gg[i][:], Gg[i][:], ACT.Ln, bias=mfl_c[:]).then_inc(ml_r, 1)
                        act.wait_ge(ml_r, at(b, 2, i + 1))
                        A(Gg[i][:], Gg[i][:], ACT.Exp, scale=0.5).then_inc(m_r, 1)

                    def lru_gate(b, i):
                        s = SLAB[SEC_LG, i]
                        act.wait_ge(slab, at(b, NS, s + 1))
                        if i == 0:
                            act.wait_ge(m2_r, at(b, 2, 2))
                        else:
                            act.wait_ge(yl_st, at(b, 32, 16))
                        A(SG[:], prod[s % 2][:], ACT.Sigmoid).then_inc(slg_r, 1)

                    def store_lru(b, i):
                        m = known(act, b * 2 + i)
                        act.wait_ge(yl_r, at(b, 2, i + 1))
                        act.dma_start(y_v[:, bass.ds(m, 1), :].rearrange("p m t -> p (m t)"), SG[:]).then_inc(yl_st, 16)

                    def block_act(b, last):
                        loaded[0] = None
                        gate_weights_high(b)
                        first_tap(b, 0); high_part(b, 3)
                        conv_high(b, 0)
                        first_tap(b, 1); high_part(b, 4)
                        conv_high(b, 1)
                        table(SIGMOID)
                        lru_gates(b, 0)
                        forget_gate(b, 0)
                        lru_gates(b, 1)
                        high_part(b, 5)
                        table(LOG_EXP)
                        log_f(b, 0)
                        lru_decay(b, 0)
                        exps(b, 0, 1); exps(b, 0, 2); chunk_decay(b, 0)
                        lru_decay(b, 1)
                        lru_input(b, 0)
                        table(SIGMOID)
                        query_gate(b, 0); high_part(b, 6)
                        table(LOG_EXP)
                        lru_input(b, 1)
                        exps(b, 0, 3)
                        keys_by_token(b, 0)
                        exps(b, 0, 4)
                        values(b, 0); high_part(b, 7)
                        values_by_token(b, 0)
                        exps(b, 0, 5); exps(b, 0, 6); exps(b, 0, 7); exps(b, 0, 8)
                        table(SIGMOID)
                        forget_gate(b, 1); high_part(b, 8)
                        table(LOG_EXP)
                        log_f(b, 1); exps(b, 1, 1); exps(b, 1, 2); chunk_decay(b, 1)
                        table(SIGMOID)
                        query_gate(b, 1); high_part(b, 9)
                        table(LOG_EXP)
                        square_out(b, 0)
                        head_rstd(b, 0)
                        exps(b, 1, 3)
                        values(b, 1); high_part(b, 10)
                        keys_by_token(b, 1)
                        exps(b, 1, 4)
                        values_by_token(b, 1)
                        exps(b, 1, 5); exps(b, 1, 6); exps(b, 1, 7); exps(b, 1, 8)
                        table(SIGMOID)
                        lru_gate(b, 0); high_part(b, 11)
                        store_lru(b, 0)
                        lru_gate(b, 1)
                        if not last:
                            high_part(b, 12)
                        head_gate(b, 0)
                        if not last:
                            high_part(b, 13)
                        store_lru(b, 1)
                        table(LOG_EXP)
                        square_out(b, 1)
                        head_rstd(b, 1)
                        table(SIGMOID)
                        head_gate(b, 1)
                        if not last:
                            high_part(b, 14)

                    with act.Fori(0, NB - 1) as b:
                        block_act(b, False)
                    block_act(NB - 1, True)
                    act.wait_ge(yl_st, at(NB, 32, 0))

                @blk.vector
                def _(dve):
                    start_full(dve, PER_DVE)
                    V_ = nc.vector
                    TT, TS, STT = V_.tensor_tensor, V_.tensor_scalar, V_.scalar_tensor_tensor

                    for t in range(NT):
                        if t == 0:
                            dve.wait_ge(pw_land, 16)
                        dve.wait_ge(x_rst, t + 1)
                        STT(out=xstage[t % 4][:], in0=xstage[t % 4][:], scalar=rst[:, t:t + 1], in1=pwb[:],
                            op0=ALU.mult, op1=ALU.mult).then_inc(x_scaled, 1)
                        if t >= 1:
                            dve.wait_ge(u_hi, t)
                            TT(ulo[:, :, (t - 1) * P:t * P], chunks(mix[(t - 1) % 2]), uhi[:, :, (t - 1) * P:t * P],
                               ALU.subtract).then_inc(u_lo, 1)
                    dve.wait_ge(u_hi, NT)
                    TT(ulo[:, :, T - P:], chunks(mix[(NT - 1) % 2]), uhi[:, :, T - P:], ALU.subtract).then_inc(u_lo, 1)

                    n = [0]

                    def step(ins):
                        n[0] += 1
                        ins.then_inc(p_dve, 1)
                        dve.wait_ge(p_dve, n[0])

                    def tmp(i):
                        return der[:, TMP + i]

                    dve.wait_ge(p_T, 1)
                    step(V_.tensor_copy(par[:], prod[1][:, 0:NPAR * KD].rearrange("p (r j) -> p r j", j=KD)))
                    TT(tmp(3), par[:, LB0], par[:, LB1], ALU.max).then_inc(p_dve, 1)
                    n[0] += 1
                    step(TS(tmp(4), par[:, LAM], -1.0, None, ALU.mult))
                    TT(tmp(0), par[:, LB0], tmp(3), ALU.subtract)
                    TT(tmp(1), par[:, LB1], tmp(3), ALU.subtract)
                    step(TT(tmp(2), par[:, LAM], tmp(4), ALU.max))
                    dve.wait_ge(p_act, 3)
                    step(TT(tmp(3), tmp(0), tmp(1), ALU.add))
                    step(V_.reciprocal(tmp(3), tmp(3)))
                    TT(der[:, LBC], tmp(0), tmp(3), ALU.mult)
                    step(TT(der[:, OML], tmp(1), tmp(3), ALU.mult))
                    step(TS(der[:, LBC], der[:, LBC], F_FLOOR, None, ALU.max))
                    step(TS(der[:, NOML], der[:, OML], -1.0, None, ALU.mult))
                    step(TS(tmp(5), tmp(2), 2.0, None, ALU.add))
                    step(V_.reciprocal(tmp(5), tmp(5)))
                    step(TT(tmp(5), tmp(5), tmp(2), ALU.mult))
                    step(TT(tmp(6), tmp(5), tmp(5), ALU.mult))
                    step(TS(tmp(7), tmp(6), 1.0 / 19, 1.0 / 17, ALU.mult, ALU.add))
                    for k in range(15, 0, -2):
                        step(TT(tmp(7), tmp(7), tmp(6), ALU.mult))
                        step(TS(tmp(7), tmp(7), 1.0 / k, None, ALU.add))
                    step(TT(tmp(7), tmp(7), tmp(5), ALU.mult))
                    step(TS(tmp(4), tmp(4), 0.0, LRU_C, ALU.max, ALU.mult))
                    step(STT(out=der[:, C8], in0=tmp(7), scalar=2.0 * LRU_C, in1=tmp(4), op0=ALU.mult, op1=ALU.add))
                    step(TS(der[:, NC8], der[:, C8], -1.0, None, ALU.mult))
                    dve.wait_ge(c_const, 1)
                    V_.memset(gate[:], 0.0).then_inc(p_par, 1)

                    def key(b, h):
                        dve.wait_ge(lf_r, at(b, 2, h + 1))
                        TS(K[h][:], K[h][:], col(der, NOML, b * 2 + h), col(der, OML, b * 2 + h),
                           ALU.mult, ALU.add).then_inc(k_r, 1)
                        V_.tensor_tensor_scan(Bs[:], keep[:], Bs[:], 0.0, ALU.mult, ALU.add).then_inc(b_r, 1)

                    def diff(b, h, j):
                        w, ref = {1: (P, P - 1), 6: (SUB, SUB // 2 - 1)}.get(j) or (2 * LEVELS[j - 2], LEVELS[j - 2] - 1)
                        dve.wait_ge(b_r, at(b, 2, h + 1))
                        dve.wait_ge(e_r, at(b, 16, 8 * h + {1: -3, 2: 0}.get(j, j - 2)))
                        bv = chunks(Bs, w)
                        TT(chunks(Dt[(j - 1) % 2], w), bv, bv[:, :, ref:ref + 1].to_broadcast([P, T // w, w]),
                           ALU.subtract).then_inc(d_r, 1)

                    def prod_e(b, h, n):
                        e = Et[(n - 1) % 2]
                        dve.wait_ge(e_r, at(b, 16, 8 * h + n))
                        if n == 1:
                            dve.wait_ge(k_r, at(b, 2, h + 1))
                            dve.wait_ge(pe_u, at(b, 2, h))
                            TT(KE[:], K[h][:], e[:], ALU.mult).then_inc(x_r, 1)
                        elif n <= 5:
                            l = LEVELS[n - 2]
                            dve.wait_ge(q_r, at(b, 2, h + 1))
                            dve.wait_ge(pe_dg, at(b, 2, h))
                            dve.wait_ge(pe_g, at(b, 4, 4))
                            xv, ev = chunks(X4[n - 2], 2 * l), chunks(e, 2 * l)
                            TT(xv[:, :, 0:l], chunks(K[h], 2 * l)[:, :, 0:l], ev[:, :, 0:l], ALU.mult)
                            TT(xv[:, :, l:], chunks(Q[h], 2 * l)[:, :, l:], ev[:, :, l:], ALU.mult).then_inc(x_r, 1)
                        elif n == 6:
                            dve.wait_ge(pe_o, at(b, 2, h))
                            TT(QE[:], Q[h][:], e[:], ALU.mult).then_inc(x_r, 1)
                        else:
                            dve.wait_ge(pe_l, at(b, 8, 4 * h + n - 6))
                            TT(X4[n - 7][:], (Q, K)[n - 7][h][:], e[:], ALU.mult).then_inc(x_r, 1)

                    def query(b, h):
                        dve.wait_ge(sq_r, at(b, 2, h + 1))
                        TT(Q[h][:], Q[h][:], prod[SLAB[SEC_Q, h] % 2][:], ALU.mult).then_inc(q_r, 1)

                    def states(b, h):
                        dve.wait_ge(pe_u, at(b, 2, h + 1))
                        dve.wait_ge(pe_o, at(b, 2, h))
                        dve.wait_ge(dec_r, at(b, 2, h + 1))
                        V_.tensor_copy(ST[:, 1], mix[0][:, 0:P]).then_inc(st_r, 1)
                        for c in range(1, NC - 1):
                            dve.wait_ge(st_r, at(b, 14, 7 * h + c))
                            STT(out=ST[:, c + 1], in0=ST[:, c], scalar=dec[:, c:c + 1], in1=mix[0][:, c * P:(c + 1) * P],
                                op0=ALU.mult, op1=ALU.add).then_inc(st_r, 1)

                    def scores(b, h, i):
                        dve.wait_ge(sc_r, at(b, 10, 5 * h + i))
                        if i == 0:
                            dve.wait_ge(pe_o, at(b, 2, h))
                        if i < 4:
                            dve.wait_ge(pe_l, at(b, 8, 4 * h + i + 1))
                        else:
                            dve.wait_ge(pe_dg, at(b, 2, h + 1))
                        V_.memset(gate[:], 0.0)
                        m = mix[(1, 0, 1, 0, 1)[i]]
                        if i < 4:
                            l = LEVELS[i]
                            nb = P // (2 * l)
                            V_.copy_predicated(S[:].rearrange("p c (i t) -> p c i t", t=2 * l)[:, :, :, l:],
                                               maskl[i][:].to_broadcast([P, NC, nb, l]),
                                               m[:, 0:HALF].rearrange("p (c i t) -> p c i t", c=NC, t=l)).then_inc(sc_r, 1)
                        else:
                            V_.copy_predicated(S[:], maskd[:].to_broadcast([P, NC, P]), chunks(m)).then_inc(sc_r, 1)

                    def norm(b, h):
                        dve.wait_ge(rs_r, at(b, 2, h + 1))
                        dve.wait_ge(x_r, at(b, 16, 8 * h + 8))
                        STT(out=Q[h][:], in0=mix[0][:], scalar=col(par, GN, b * 2 + h), in1=G[:],
                            op0=ALU.mult, op1=ALU.mult).then_inc(z_r, 1)

                    def gate_out(b, h):
                        dve.wait_ge(shg_r, at(b, 2, h + 1))
                        TT(V[h][:], V[h][:], prod[SLAB[SEC_HG, h] % 2][:], ALU.mult).then_inc(hg_r, 1)

                    def head_out(b, h):
                        dve.wait_ge(hg_r, at(b, 2, h + 1))
                        dve.wait_ge(z_r, at(b, 2, h + 1))
                        TT(V[h][:], V[h][:], Q[h][:], ALU.mult).then_inc(y_r, 1)

                    def conv(b, i):
                        dve.wait_ge(xt_r, at(b, 2, i + 1))
                        src = prod[SLAB[SEC_X, i] % 2]
                        for d in range(1, 4):
                            if d > 1:
                                dve.wait_ge(cv_r, at(b, 6, 3 * i + d - 1))
                            STT(out=XC[i][:, d:], in0=src[:, 0:T - d], scalar=col(par, CW + 3 - d, b * 2 + i),
                                in1=XC[i][:, d:], op0=ALU.mult, op1=ALU.add).then_inc(cv_r, 1)

                    def gate_weights_low(b):
                        dve.wait_ge(gwh_r, at(b, 1, 1))
                        dve.wait_ge(pe_o, at(b, 2, 0))
                        TT(gwl[:], gw[:], gwh[:], ALU.subtract).then_inc(gwl_r, 1)

                    def conv_low(b, i):
                        dve.wait_ge(xh_r, at(b, 2, i + 1))
                        dve.wait_ge(pe_l, at(b, 8, 0))
                        TT(xcl[i][:], XC[i][:], xch[i][:], ALU.subtract).then_inc(xl_r, 1)

                    def square_low(b, h):
                        dve.wait_ge(o2h_r, at(b, 2, h + 1))
                        dve.wait_ge(pe_ms, at(b, 2, h))
                        TT(o2l[:], G[:], o2h[:], ALU.subtract).then_inc(o2l_r, 1)

                    def gated_input(b, i):
                        dve.wait_ge(i_r, at(b, 2, i + 1))
                        TT(Ig[i][:], Ig[i][:], XC[i][:], ALU.mult).then_inc(ix_r, 1)

                    def lru_factor(b, i):
                        dve.wait_ge(a2_r, at(b, 2, i + 1))
                        STT(out=Gg[i][:], in0=SG[:], scalar=1.0, in1=Gg[i][:], op0=ALU.add, op1=ALU.mult).then_inc(m2_r, 1)

                    def lru_scan(b, i):
                        dve.wait_ge(m_r, at(b, 2, i + 1))
                        dve.wait_ge(ix_r, at(b, 2, i + 1))
                        TT(Ig[i][:], Ig[i][:], Gg[i][:], ALU.mult).then_inc(lu_r, 1)
                        dve.wait_ge(lu_r, at(b, 2, i + 1))
                        dve.wait_ge(xh_r, at(b, 2, i + 1))
                        V_.tensor_tensor_scan(XC[i][:], Rg[i][:], Ig[i][:], 0.0, ALU.mult, ALU.add).then_inc(h_r, 1)

                    def lru_out(b, i):
                        dve.wait_ge(slg_r, at(b, 2, i + 1))
                        TT(SG[:], SG[:], prod[SLAB[SEC_LG, i] % 2][:], ALU.mult).then_inc(lg_r, 1)
                        dve.wait_ge(lg_r, at(b, 2, i + 1))
                        dve.wait_ge(h_r, at(b, 2, i + 1))
                        TT(SG[:], SG[:], XC[i][:], ALU.mult).then_inc(yl_r, 1)

                    def block_dve(b):
                        gate_weights_low(b)
                        conv(b, 0); conv_low(b, 0)
                        conv(b, 1); conv_low(b, 1)
                        gated_input(b, 0)
                        gated_input(b, 1)
                        key(b, 0); diff(b, 0, 1); diff(b, 0, 2)
                        lru_factor(b, 0)
                        prod_e(b, 0, 1)
                        lru_factor(b, 1)
                        diff(b, 0, 3)
                        lru_scan(b, 0)
                        query(b, 0)
                        prod_e(b, 0, 2)
                        diff(b, 0, 4); prod_e(b, 0, 3)
                        lru_scan(b, 1)
                        diff(b, 0, 5); prod_e(b, 0, 4)
                        diff(b, 0, 6); prod_e(b, 0, 5)
                        prod_e(b, 0, 6)
                        states(b, 0)
                        scores(b, 0, 0); prod_e(b, 0, 7)
                        scores(b, 0, 1); prod_e(b, 0, 8)
                        scores(b, 0, 2)
                        scores(b, 0, 3)
                        scores(b, 0, 4)
                        key(b, 1); diff(b, 1, 1); diff(b, 1, 2); prod_e(b, 1, 1)
                        query(b, 1)
                        square_low(b, 0)
                        diff(b, 1, 3); prod_e(b, 1, 2)
                        norm(b, 0)
                        diff(b, 1, 4); prod_e(b, 1, 3)
                        diff(b, 1, 5); prod_e(b, 1, 4)
                        diff(b, 1, 6); prod_e(b, 1, 5)
                        prod_e(b, 1, 6)
                        states(b, 1)
                        scores(b, 1, 0); prod_e(b, 1, 7)
                        lru_out(b, 0)
                        scores(b, 1, 1); prod_e(b, 1, 8)
                        scores(b, 1, 2)
                        lru_out(b, 1)
                        scores(b, 1, 3)
                        scores(b, 1, 4)
                        gate_out(b, 0)
                        head_out(b, 0)
                        square_low(b, 1)
                        norm(b, 1)
                        gate_out(b, 1)
                        head_out(b, 1)

                    with dve.Fori(0, NB - 1) as b:
                        block_dve(b)
                    block_dve(NB - 1)

                @blk.tensor
                def _(pe):
                    start_full(pe, PER_PE)
                    M = nc.tensor.matmul

                    pe.wait_ge(c_pool, 2)
                    for t in range(NT):
                        pe.wait_ge(x_scaled, t + 1)
                        if t >= 2:
                            pe.wait_ge(u_lo, t - 1)
                        for k in range(KD):
                            last = nc.tensor.transpose(mix[t % 2][:, k * P:(k + 1) * P], xstage[t % 4][:, k * P:(k + 1) * P], ident[:])
                        last.then_inc(x_tr, 1)
                        if t == 1:
                            pe.wait_ge(p_land, 16 * 7)
                            n = NPAR * KD
                            nc.tensor.transpose(prod[1][:, 0:n], prow[0:n, 0:P], ident[0:n, 0:n]).then_inc(p_T, 1)
                    pe.wait_ge(u_lo, NT)
                    pe.wait_ge(p_dve, 1)

                    frees = {SEC_F: (sf_r, 2, 1), SEC_Q: (q_r, 2, 1), SEC_V: (v_r, 2, 1), SEC_X: (cv_r, 6, 3),
                             SEC_HG: (hg_r, 2, 1), SEC_LG: (lg_r, 2, 1)}

                    def product(b, s):
                        pe.wait_ge(w_lo, at(b, NS, s + 1))
                        sec, j = SLABS[s - 2]
                        fs, per, each = frees[sec]
                        pe.wait_ge(fs, at(b, per, each * (j + 1) - (per if s < 2 else 0)))
                        hi, lo = whi[s % SLOTS], wlo[s % SLOTS]
                        n = 0
                        for half in range(2):
                            t = slice(half * HALF, (half + 1) * HALF)
                            for k in range(KD):
                                for w, u in ((hi, uhi), (hi, ulo), (lo, uhi)):
                                    last = M(prod[s % 2][:, t], w[:, k], u[:, k, t], start=(n % 24 == 0), stop=(n % 24 == 23))
                                    n += 1
                                    if n % 12 == 0:
                                        if n == 48:
                                            last.then_inc(slab, 1)
                                        for name, arg in WHEN.get(4 * s + n // 12 - 1, []):
                                            step(b, name, arg)

                    def step(b, name, h):
                        c_ = [slice(c * P, (c + 1) * P) for c in range(NC)]
                        if name == "tk":
                            pe.wait_ge(x_r, at(b, 16, 8 * h + 1))
                            pe.wait_ge(*((r_r, at(b, 2, 2)) if h == 0 else (z_r, at(b, 2, 1))))
                            for c in range(NC):
                                last = nc.tensor.transpose(mix[0][:, c_[c]], KE[:, c_[c]], ident[:])
                            last.then_inc(pe_tk, 1)
                        elif name == "tv":
                            pe.wait_ge(v_r, at(b, 2, h + 1))
                            pe.wait_ge(*((i_r, at(b, 2, 2)) if h == 0 else (ln_r, at(b, 2, 1))))
                            for c in range(NC):
                                last = nc.tensor.transpose(mix[1][:, c_[c]], V[h][:, c_[c]], ident[:])
                            last.then_inc(pe_tv, 1)
                        elif name == "u":
                            pe.wait_ge(kt_r, at(b, 2, h + 1))
                            pe.wait_ge(vt_r, at(b, 2, h + 1))
                            for c in range(NC - 1):
                                last = M(mix[0][:, c_[c]], KE[:, c_[c]], V[h][:, c_[c]], start=True, stop=True)
                            last.then_inc(pe_u, 1)
                        elif name[0] == "l":
                            i = int(name[1])
                            l = LEVELS[i]
                            pe.wait_ge(x_r, at(b, 16, 8 * h + 2 + i))
                            pe.wait_ge(*((vt_r, at(b, 2, h + 1)), (st_r, at(b, 14, 7 * (h + 1))),
                                         (sc_r, at(b, 10, 5 * h + 1)), (sc_r, at(b, 10, 5 * h + 2)))[i])
                            for c in range(NC):
                                second = X4[i][:, c_[c]].rearrange("p (i t) -> p i t", t=2 * l)[:, :, l:]
                                last = M(mix[(1, 0, 1, 0)[i]][:, c * 64:(c + 1) * 64], X4[i][:, c_[c]], second,
                                         start=True, stop=True)
                            last.then_inc(pe_l, 1)
                        elif name == "dg":
                            pe.wait_ge(x_r, at(b, 16, 8 * h + 8))
                            pe.wait_ge(sc_r, at(b, 10, 5 * h + 3))
                            for c in range(NC):
                                last = M(mix[1][:, c_[c]], X4[1][:, c_[c]], X4[0][:, c_[c]], start=True, stop=True)
                            last.then_inc(pe_dg, 1)
                        elif name == "o":
                            pe.wait_ge(x_r, at(b, 16, 8 * h + 6))
                            pe.wait_ge(sc_r, at(b, 10, 5 * h + 5))
                            pe.wait_ge(st_r, at(b, 14, 7 * (h + 1)))
                            for c in range(NC):
                                last = M(mix[0][:, c_[c]], V[h][:, c_[c]], S[:, c], start=True, stop=(c == 0))
                                if c:
                                    last = M(mix[0][:, c_[c]], ST[:, c], QE[:, c_[c]], start=False, stop=True)
                            last.then_inc(pe_o, 1)
                        elif name == "ms":
                            pe.wait_ge(o2l_r, at(b, 2, h + 1))
                            for half in range(2):
                                t = slice(half * HALF, (half + 1) * HALF)
                                M(mix[1][:, t], ones[:], o2h[:, t], start=True, stop=False)
                                last = M(mix[1][:, t], ones[:], o2l[:, t], start=False, stop=True)
                            last.then_inc(pe_ms, 1)
                        elif name == "g":
                            i, gate_ = h // 2, h % 2
                            pe.wait_ge(gwl_r, at(b, 1, 1))
                            pe.wait_ge(xl_r, at(b, 2, 2))
                            pe.wait_ge(*((z_r, at(b, 2, 0)), (ln_r, at(b, 2, 0)), (r_r, at(b, 2, 1)), (i_r, at(b, 2, 1)))[h])
                            for half in range(2):
                                t = slice(half * HALF, (half + 1) * HALF)
                                for k in range(2):
                                    for n, (w, xc) in enumerate(((gwh, xch), (gwl, xch), (gwh, xcl))):
                                        last = M(mix[h % 2][:, t], w[:, gate_, k, i * P:(i + 1) * P], xc[k][:, t],
                                                 start=(k == 0 and n == 0), stop=(k == 1 and n == 2))
                            last.then_inc(pe_g, 1)

                    with pe.Fori(0, NB - 1) as b:
                        for s in range(NS):
                            product(b, s)
                    for s in range(NS):
                        product(NB - 1, s)

        GT = 2 * P
        NG = T // GT
        order = [m for m0, m1 in PIECES for m in range(m0, m1)]
        NPC = len(PIECES)
        wr_land = [sem(f"wr_land{i}") for i in range(2)]
        yr_land = [sem(f"yr_land{i}") for i in range(NPC)]
        xr_land = [sem(f"xr_land{i}") for i in range(2)]
        po_st = [sem(f"po_st{i}") for i in range(2)]
        (pw2_land, wo_hi, wo_lo, yh_r, yl2_r, pe_pc, pe_grp, sq2_r, ln2_r, rs2_r, o1_r, o2o_r) = [sem(n) for n in (
            "pw2_land wo_hi wo_lo yh_r yl2_r pe_pc pe_grp sq2_r ln2_r rs2_r o1_r o2o_r").split()]
        with ExitStack() as octx:
            def ob(name, shape, dt=F32):
                return octx.enter_context(nc.sbuf_tensor(name, shape, dt))

            WH, WL = ob("WH", [P, MT, D], F32R), ob("WL", [P, MT, D], F32R)
            YH, YL = ob("YH", [P, MT, GT], F32R), ob("YL", [P, MT, GT], F32R)
            YR = ob("YR", [P, MT, GT])
            WR = [ob(f"WR{i}", [P, D]) for i in range(2)]
            pwo = ob("pwo", [P, D])
            XR = [ob(f"XR{i}", [P, D]) for i in range(2)]
            OT = [ob(f"OT{i}", [P, D]) for i in range(2)]

            x_v = x[0].rearrange("(t p) d -> t p d", p=P)
            o_v = out[0].rearrange("(t p) d -> t p d", p=P)
            wo_v = w_out[0].rearrange("(m p) d -> m p d", p=P)
            y_g = y_scr.rearrange("m p (g t) -> p g m t", t=GT)

            with nc.Block() as blk:
                @blk.sync
                def _(sp):
                    for eng_, per in ((sp, {yh_r: NPC, yl2_r: NPC, pe_pc: NPC, pe_grp: 1, o1_r: 2, o2o_r: 2, sq2_r: 2,
                                            ln2_r: 2, rs2_r: 2, po_st[0]: 16, po_st[1]: 16}),):
                        start_full(eng_, per)
                    sp.dma_start(pwo[:], post_norm_w.to_broadcast([P, D])).then_inc(pw2_land, 16)

                    def load_w(i):
                        if i >= 2:
                            sp.wait_ge(wo_lo, i - 1)
                        sp.dma_start(WR[i % 2][:], wo_v[order[i]]).then_inc(wr_land[i % 2], 16)

                    def load_y(g, p):
                        m0, m1 = PIECES[p]
                        sp.dma_start(YR[:, m0:m1, :], y_g[:, g, m0:m1, :]).then_inc(yr_land[p], 16)

                    load_w(0); load_y(0, 0); load_w(1); load_y(0, 1)
                    for i in range(2, MT):
                        load_w(i)
                        if i == 3:
                            load_y(0, 2); load_y(0, 3)
                            for j in range(2):
                                sp.dma_start(XR[j][:], x_v[j]).then_inc(xr_land[j], 16)
                    for g in range(NG):
                        if g + 1 < NG:
                            for p in range(NPC):
                                sp.wait_ge(yl2_r, at(g, NPC, p + 1))
                                load_y(g + 1, p)
                        for j in range(2):
                            sp.wait_ge(o2o_r, at(g, 2, j + 1))
                            sp.dma_start(o_v[2 * g + j], OT[j][:]).then_inc(po_st[j], 16)
                            if g + 1 < NG:
                                sp.dma_start(XR[j][:], x_v[2 * g + 2 + j]).then_inc(xr_land[j], 16)
                    for j in range(2):
                        sp.wait_ge(po_st[j], at(NG, 16, 0))

                @blk.scalar
                def _(act):
                    A = nc.scalar.activation

                    def y_high(g, p):
                        m0, m1 = PIECES[p]
                        act.wait_ge(yr_land[p], 16 * (g + 1))
                        act.wait_ge(pe_pc, at(g, NPC, p + 1 - NPC))
                        A(YH[:, m0:m1], YR[:, m0:m1], ACT.Copy).then_inc(yh_r, 1)

                    def w_high(i):
                        act.wait_ge(wr_land[i % 2], 16 * (i // 2 + 1))
                        A(WH[:, order[i]], WR[i % 2][:], ACT.Copy).then_inc(wo_hi, 1)

                    def rstd(g, j):
                        acc = (prod, mix)[g % 2][j]
                        c = 2 * g + j
                        if j == 0:
                            act.wait_ge(pe_grp, at(g, 1, 1))
                        else:
                            act.wait_ge(pe_pc, at(g, NPC, NPC))
                        act.wait_ge(po_st[j], at(g, 16, 0))
                        A(OT[j][:], acc[:], ACT.Square, accum_out=ssq[:, c:c + 1]).then_inc(sq2_r, 1)
                        act.wait_ge(sq2_r, at(g, 2, j + 1))
                        A(rst[:, c:c + 1], ssq[:, c:c + 1], ACT.Ln, scale=1.0 / D, bias=eps_c[:]).then_inc(ln2_r, 1)
                        act.wait_ge(ln2_r, at(g, 2, j + 1))
                        A(rst[:, c:c + 1], rst[:, c:c + 1], ACT.Exp, scale=-0.5).then_inc(rs2_r, 1)

                    w_high(0); y_high(0, 0)
                    for i in range(1, MT):
                        w_high(i)
                        if i in (2, 4, 6):
                            y_high(0, i // 2)
                    for g in range(NG):
                        if g + 1 < NG:
                            y_high(g + 1, 0)
                            y_high(g + 1, 1)
                            y_high(g + 1, 2)
                        rstd(g, 0)
                        rstd(g, 1)
                        if g + 1 < NG:
                            y_high(g + 1, 3)

                @blk.vector
                def _(dve):
                    TT = nc.vector.tensor_tensor

                    def y_low(g, p):
                        m0, m1 = PIECES[p]
                        dve.wait_ge(yh_r, at(g, NPC, p + 1))
                        TT(YL[:, m0:m1], YR[:, m0:m1], YH[:, m0:m1], ALU.subtract).then_inc(yl2_r, 1)

                    def w_low(i):
                        dve.wait_ge(wo_hi, i + 1)
                        TT(WL[:, order[i]], WR[i % 2][:], WH[:, order[i]], ALU.subtract).then_inc(wo_lo, 1)

                    def finish(g, j):
                        acc = (prod, mix)[g % 2][j]
                        c = 2 * g + j
                        dve.wait_ge(rs2_r, at(g, 2, j + 1))
                        dve.wait_ge(pw2_land, 16)
                        nc.vector.scalar_tensor_tensor(out=OT[j][:], in0=acc[:], scalar=rst[:, c:c + 1], in1=pwo[:],
                                                       op0=ALU.mult, op1=ALU.mult).then_inc(o1_r, 1)
                        dve.wait_ge(o1_r, at(g, 2, j + 1))
                        dve.wait_ge(xr_land[j], 16 * (g + 1))
                        TT(OT[j][:], OT[j][:], XR[j][:], ALU.add).then_inc(o2o_r, 1)

                    w_low(0); y_low(0, 0)
                    for i in range(1, MT):
                        w_low(i)
                        if i in (2, 4, 6):
                            y_low(0, i // 2)
                    for g in range(NG):
                        if g + 1 < NG:
                            y_low(g + 1, 0)
                            y_low(g + 1, 1)
                            y_low(g + 1, 2)
                        finish(g, 0)
                        finish(g, 1)
                        if g + 1 < NG:
                            y_low(g + 1, 3)

                @blk.tensor
                def _(pe):
                    M = nc.tensor.matmul
                    for g in range(NG):
                        acc = (prod, mix)[g % 2]
                        i = 0
                        if g >= 2:
                            pe.wait_ge(o1_r, at(g, 2, -2))
                        for p, (m0, m1) in enumerate(PIECES):
                            pe.wait_ge(yl2_r, at(g, NPC, p + 1))
                            for m in range(m0, m1):
                                if g == 0:
                                    pe.wait_ge(wo_lo, i + 1)
                                for j in range(2):
                                    tok = slice(j * P, (j + 1) * P)
                                    n = 0
                                    for y, w in ((YH, WH), (YH, WL), (YL, WH)):
                                        for half in range(2):
                                            d = slice(half * HALF, (half + 1) * HALF)
                                            last = M(acc[j][:, d], y[:, m, tok], w[:, m, d], start=(i == 0 and n < 2),
                                                     stop=(i == MT - 1 and n >= 4))
                                            n += 1
                                    if i == MT - 1 and j == 0:
                                        last.then_inc(pe_grp, 1)
                                i += 1
                            last.then_inc(pe_pc, 1)


INS = ["x", "pre_norm_w", "w_in", "conv_w", "conv_b", "lru_w_a", "lru_b_a", "lru_w_x", "lru_b_x", "lru_lambda",
       "hgrn_lb_logits", "hgrn_gnorm_w", "w_out", "post_norm_w"]


def kernel(**inputs):
    import numpy as np
    import concourse.bacc as bacc
    from concourse.bass_utils import run_bass_kernel_spmd

    nc = bacc.Bacc("TRN2", target_bir_lowering=False, num_devices=1)
    arrays, args = {}, []
    for name in INS:
        a = np.ascontiguousarray(inputs[name])
        arrays[f"in_{name}"] = a
        args.append(nc.dram_tensor(f"in_{name}", a.shape, mybir.dt.from_np(a.dtype), kind="ExternalInput").ap())
    _, seq, width = inputs["x"].shape
    out = nc.dram_tensor("out_h", (1, seq, width), F32, kind="ExternalOutput").ap()
    scratch = nc.dram_tensor("mixed", (inputs["w_out"].shape[1] // P, P, seq), F32, kind="Internal").ap()
    build(nc, *args, out, scratch)
    r = run_bass_kernel_spmd(nc, [arrays], core_ids=[0])
    return r.results[0]["out_h"]
```

```python
from contextlib import ExitStack

import concourse.bass as bass
from concourse import mybir

F32 = mybir.dt.float32
F32R = mybir.dt.float32r
I8 = mybir.dt.int8
ALU = mybir.AluOpType
ACT = mybir.ActivationFunctionType

P = 128
EPS = 1e-6
F_FLOOR = 1e-9
M_FLOOR = 2.0 ** -60
LRU_C = 8.0
LEVELS = (64, 32, 16, 8)
SUB = 8
HALF = 512
SLOTS = 3

CW, CB, BA, BX, LAM, LB0, LB1, GN = 0, 4, 5, 6, 7, 8, 9, 10
NPAR = 11
LBC, OML, NOML, C8, NC8, TMP = 0, 1, 2, 3, 4, 5
NDER = 13

SEC_X, SEC_LG, SEC_Q, SEC_F, SEC_V, SEC_HG = range(6)
SLABS = [(SEC_X, 0), (SEC_X, 1), (SEC_F, 0), (SEC_Q, 0), (SEC_V, 0), (SEC_V, 1), (SEC_F, 1), (SEC_Q, 1),
         (SEC_LG, 0), (SEC_LG, 1), (SEC_HG, 0), (SEC_HG, 1)]
NS = len(SLABS)
SLAB = {sj: s for s, sj in enumerate(SLABS)}

WHEN = {11: [("g", _n) for _n in range(4)]}
for _h, _qs in enumerate([(17, 21, 22, 23, 24, 25, 26, 28, 30), (33, 35, 36, 37, 38, 39, 40, 42, 44)]):
    for _s, _q in zip(["tk", "l0", "l1", "l2", "l3", "dg", "u", "o", "ms"], _qs):
        WHEN.setdefault(_q, []).append((_s, _h))

PIECES = [(0, 6), (8, 14), (6, 8), (14, 16)]


def at(b, per, n):
    return (b + 1) * per + n


def build(nc, x, pre_norm_w, w_in, conv_w, conv_b, lru_w_a, lru_b_a, lru_w_x, lru_b_x, lru_lambda,
          hgrn_lb_logits, hgrn_gnorm_w, w_out, post_norm_w, out, y_scr):
    T, D = x.shape[1], x.shape[2]
    NT, KD, MT = T // P, D // P, w_out.shape[1] // P
    NB, NC = KD // 2, T // P
    assert T == 1024 and D == 1024 and MT == 2 * KD

    ctx = ExitStack()
    with ctx:
        def sem(name):
            return ctx.enter_context(nc.semaphore(name))

        def sb(name, shape, dt=F32, c=ctx):
            return c.enter_context(nc.sbuf_tensor(name, shape, dt))

        ident = sb("ident", [P, P])
        ones = sb("ones", [P, P], F32R)
        maskl = {l: sb(f"mask{l}", [P, 1, P // (2 * l), l], I8) for l in LEVELS[1:]}
        maskd = sb("maskd", [P, 1, P], I8)
        keep = sb("keep", [P, T], I8)
        eps_c = sb("eps_c", [P, 1])
        mfl_c = sb("mfl_c", [P, 1])
        par = sb("par", [P, NPAR, KD])
        der = sb("der", [P, NDER, KD])
        dec = sb("dec", [P, NC])
        ssq = sb("ssq", [P, NT + 1])
        rst = sb("rst", [P, NT])
        eps2 = sb("eps2", [P, 1])
        gate = sb("gate", [1, 1])

        prod = [ctx.enter_context(nc.psum_tensor(f"prod{i}", [P, T], F32)) for i in range(2)]
        mix = [ctx.enter_context(nc.psum_tensor(f"mix{i}", [P, T], F32)) for i in range(2)]

        c_pool, c_const, p_land, p_T, p_par, p_dve, p_act, pw_land = [sem(n) for n in (
            "c_pool c_const p_land p_T p_par p_dve p_act pw_land").split()]
        x_land = [sem(f"x_land{t}") for t in range(NT)]
        x_ssq, x_ln, x_rst, x_scaled, x_tr, u_hi, u_lo = [sem(n) for n in (
            "x_ssq x_ln x_rst x_scaled x_tr u_hi u_lo").split()]
        w_land = [sem(f"w_land{i}") for i in range(2)]
        wx_land = [sem(f"wx_land{i}") for i in range(2)]
        g_land = [sem(f"g_land{i}") for i in range(2)]
        w_hi, w_hi0, w_lo, slab = sem("w_hi"), sem("w_hi0"), sem("w_lo"), sem("slab")
        sf_r, sq_r, v_r, lf_r, k_r, b_r, q_r = [sem(n) for n in "sf_r sq_r v_r lf_r k_r b_r q_r".split()]
        d_r, e_r, x_r, dec_r = [sem(n) for n in "d_r e_r x_r dec_r".split()]
        pe_tk, pe_u, pe_l, pe_dg, pe_o, pe_ms, pe_g = [sem(n) for n in "pe_tk pe_u pe_l pe_dg pe_o pe_ms pe_g".split()]
        kt_r, st_r, sc_r, o2_r, ln_r, rs_r, z_r = [sem(n) for n in "kt_r st_r sc_r o2_r ln_r rs_r z_r".split()]
        shg_r, hg_r, y_r = [sem(n) for n in "shg_r hg_r y_r".split()]
        gwh_r, gwl_r, xh_r, xl_r, o2h_r, o2l_r = [sem(n) for n in "gwh_r gwl_r xh_r xl_r o2h_r o2l_r".split()]
        xt_r, cv_r, r_r, i_r, th_r, a_r, a2_r, m2_r, ml_r, m_r = [sem(n) for n in (
            "xt_r cv_r r_r i_r th_r a_r a2_r m2_r ml_r m_r").split()]
        ix_r, lu_r, h_r, slg_r, lg_r, yl_r = [sem(n) for n in "ix_r lu_r h_r slg_r lg_r yl_r".split()]
        yh_st = [sem(f"yh_st{i}") for i in range(2)]
        yl_st = sem("yl_st")

        PER_PE = {slab: NS, pe_tk: 2, pe_u: 2, pe_l: 8, pe_dg: 2, pe_o: 2, pe_ms: 2, pe_g: 4}
        PER_ACT = {w_hi: NS, sf_r: 2, sq_r: 2, v_r: 2, lf_r: 2, e_r: 16, dec_r: 2, kt_r: 2, o2_r: 2, o2h_r: 2,
                   gwh_r: 1, xh_r: 2, ln_r: 2, rs_r: 2,
                   shg_r: 2, xt_r: 2, r_r: 2, i_r: 2, th_r: 2, a_r: 2, a2_r: 2, ml_r: 2, m_r: 2, slg_r: 2, yl_st: 32}
        PER_DVE = {gwl_r: 1, xl_r: 2, o2l_r: 2, k_r: 2, b_r: 2, q_r: 2, d_r: 12, x_r: 16, st_r: 14, sc_r: 10, z_r: 2, hg_r: 2, y_r: 2,
                   cv_r: 6, m2_r: 2, ix_r: 2, lu_r: 2, h_r: 2, lg_r: 2, yl_r: 2}
        PER_POOL = {w_lo: NS}
        PER_SP = {yh_st[0]: 16, yh_st[1]: 16}

        GT = 2 * P
        NG = T // GT
        order = [m for m0, m1 in PIECES for m in range(m0, m1)]
        NPC = len(PIECES)
        PARTS = [(g, j, slice(0, D)) for g in range(NG) for j in range(2)][:-1]
        PARTS += [(NG - 1, 1, slice(0, HALF)), (NG - 1, 1, slice(HALF, D))]
        wr_land = [sem(f"wr_land{i}") for i in range(4)]
        yr_land = [sem(f"yr_land{i}") for i in range(NPC)]
        xr_land = [sem(f"xr_land{i}") for i in range(2)]
        out_st = [sem(f"out_st{i}") for i in range(2)]
        pw2_land, wo_hi, wo_lo, yh_r, yl2_r, pe_pc, pe_part, sq2_r, eb_r, ln2_r, rs2_r, o1_r, o2_done = [sem(n) for n in (
            "pw2_land wo_hi wo_lo yh_r yl2_r pe_pc pe_part sq2_r eb_r ln2_r rs2_r o1_r o2_done").split()]

        def raw_slot(i):
            return (i, 1) if i < 2 else ((i - 2) % 4, (i - 2) // 4 + (2 if (i - 2) % 4 < 2 else 1))

        def start_full(eng, per):
            for s, n in per.items():
                eng.sem_inc(s, n)

        with ExitStack() as mctx:
            def mb(name, shape, dt=F32):
                return mctx.enter_context(nc.sbuf_tensor(name, shape, dt))

            with ExitStack() as actx:
                xch = [sb(f"xch{i}", [P, T], F32R, actx) for i in range(2)]
                xcl = [sb(f"xcl{i}", [P, T], F32R, actx) for i in range(2)]
            X4 = [mb(f"X{i}", [P, T]) for i in range(4)]
            Dt = [mb(f"D{i}", [P, T]) for i in range(2)]
            Et = [mb(f"E{i}", [P, T]) for i in range(2)]
            KE = mb("KE", [P, T])
            XC = [mb(f"XC{h}", [P, T]) for h in range(2)]
            Bs = mb("Bs", [P, T])
            uhi = mb("uhi", [P, KD, T], F32R)
            ulo = mb("ulo", [P, KD, T], F32R)
            w_split = [mb(n, [P, SLOTS, KD, P], F32R) for n in ("whi", "wlo")]
            whi, wlo = [[w[:, i] for i in range(SLOTS)] for w in w_split]
            wraw = [mb(f"wraw{i}", [P, KD, P]) for i in range(2)]
            with ExitStack() as actx:
                gwh, gwl = [sb(n, [P, 2, 2, 2 * P], F32R, actx) for n in ("gwh", "gwl")]
                o2h, o2l = [sb(n, [P, T], F32R, actx) for n in ("o2h", "o2l")]
            QE = mb("QE", [P, T])
            ST = mb("ST", [P, NC, P])
            R, I = mb("R", [P, T]), mb("I", [P, T])
            gw = mb("gw", [P, 2, 2, 2 * P])
            K = [mb(f"K{h}", [P, T]) for h in range(2)]
            S = mb("S", [P, NC, P])
            G, SG = mb("G", [P, T]), mb("SG", [P, T])
            Q = [mb(f"Q{h}", [P, T]) for h in range(2)]
            V = [mb(f"V{h}", [P, T]) for h in range(2)]
            Rg, Ig, Gg = (R, K[1]), (I, Q[1]), (G, ST[:].rearrange("p c v -> p (c v)"))
            xstage = [R, I, K[0], K[1], Q[0], Q[1], V[0], V[1]]
            pwb, prow = XC[0], XC[1]


        with ExitStack() as octx:
            def ob(name, shape, dt=F32):
                return octx.enter_context(nc.sbuf_tensor(name, shape, dt))

            size = [m1 - m0 for m0, m1 in PIECES]
            WR = [ob(f"WR{i}", [P, D]) for i in range(2)]
            W0 = [ob(n, [P, 2, D], F32R) for n in ("WH0", "WL0")]
            YR = [ob(f"YR{p}", [P, size[p], GT]) for p in range(2)]
            YH, YL = [[ob(f"{n}0", [P, size[0], GT], F32R)] for n in ("YH", "YL")]
            W1 = [ob(n, [P, MT - 2, D], F32R) for n in ("WH1", "WL1")]
            for n, ys in (("YH", YH), ("YL", YL)):
                ys += [ob(f"{n}{p}", [P, size[p], GT], F32R) for p in range(1, NPC)]
            YR += [ob(f"YR{p}", [P, size[p], GT]) for p in range(2, NPC)]
            XR = [ob(f"XR{i}", [P, D]) for i in range(2)]
            OT = [ob(f"OT{i}", [P, D]) for i in range(2)]
            pwo = ob("pwo", [P, D])
            WR += XR

        x_v = x[0].rearrange("(t p) d -> t p d", p=P)
        w_v = w_in[0].rearrange("(k p) (s j c) -> p k s j c", p=P, s=6, c=P)
        ga_v = lru_w_a[0].rearrange("n (k p) c -> p n k c", p=P)
        gx_v = lru_w_x[0].rearrange("n (k p) c -> p n k c", p=P)
        y_v = y_scr.rearrange("m p t -> p m t")
        o_v = out[0].rearrange("(t p) d -> t p d", p=P)
        wo_v = w_out[0].rearrange("(m p) d -> m p d", p=P)
        y_g = y_scr.rearrange("m p (g t) -> p g m t", t=GT)

        acc = [[prod[0], mix[1]], [mix[0], prod[1]]]

        def piece_used(g, p):
            return (pe_pc, g * (NPC - 1) + p + 1) if p < NPC - 1 else (pe_part, 2 * g + 2)

        def wo_part(w, i):
            return W0[w][:, i] if i < 2 else W1[w][:, i - 2]

        def col(table, row, j):
            return table[:, row, bass.ds(j, 1)]

        def chunks(t_, w=P):
            return t_[:].rearrange("p (c t) -> p c t", t=w)

        def known(eng, v):
            return v if isinstance(v, int) else eng.snap(v)

        with nc.Block() as blk:
            @blk.sync
            def _(sp):
                start_full(sp, PER_SP)
                rows = [(conv_w[0].rearrange("k (j p) -> (k j) p", p=P), 4 * KD),
                        (conv_b.rearrange("a (j p) -> (a j) p", p=P), KD),
                        (lru_b_a[0].rearrange("n (j p) -> (n j) p", p=P), KD),
                        (lru_b_x[0].rearrange("n (j p) -> (n j) p", p=P), KD),
                        (lru_lambda.rearrange("a (j p) -> (a j) p", p=P), KD),
                        (hgrn_lb_logits.rearrange("a (j p) -> (a j) p", p=P), 2 * KD),
                        (hgrn_gnorm_w.rearrange("a (j p) -> (a j) p", p=P), KD)]

                def load_slab(s):
                    sec, j = SLABS[s]
                    sp.dma_start(wraw[s][:], w_v[:, :, sec, j, :]).then_inc(w_land[s], 16)

                sp.dma_start(xstage[0][:], x_v[0]).then_inc(x_land[0], 16)
                sp.dma_start(pwb[:], pre_norm_w.to_broadcast([P, D])).then_inc(pw_land, 16)
                sp.dma_start(xstage[1][:], x_v[1]).then_inc(x_land[1], 16)
                load_slab(0)
                for t in range(2, 4):
                    sp.dma_start(xstage[t][:], x_v[t]).then_inc(x_land[t], 16)
                n = 0
                for src, cnt in rows:
                    sp.dma_start(prow[n:n + cnt, 0:P], src).then_inc(p_land, 16)
                    n += cnt
                load_slab(1)
                for t in range(4, NT):
                    sp.dma_start(xstage[t][:], x_v[t]).then_inc(x_land[t], 16)
                for g, src in enumerate((ga_v, gx_v)):
                    sp.dma_start(gw[:, g], src[:, 0]).then_inc(g_land[g], 16)

                def load_block(b, last):
                    for k in range(2, NS if last else NS + 2):
                        sec, j = SLABS[k % NS]
                        if sec == SEC_X:
                            continue
                        jj = b * 2 + j + (2 if k >= NS else 0)
                        need = known(sp, at(b, NS, k - 1))
                        sp.wait_ge(w_lo, need)
                        sp.dma_start(wraw[k % 2][:], w_v[:, :, sec, bass.ds(jj, 1), :].rearrange("p k j c -> p k (j c)")
                                     ).then_inc(w_land[k % 2], 16)
                        if k in (8, 9) and not last:
                            src = (ga_v, gx_v)[k - 8]
                            need = known(sp, at(b, 1, 1))
                            sp.wait_ge(gwl_r, need)
                            sp.dma_start(gw[:, k - 8], src[:, bass.ds(b + 1, 1)].rearrange("p n k c -> p (n k) c")
                                         ).then_inc(g_land[k - 8], 16)
                    for h in range(0 if last else 2):
                        store_head(b, h)

                def store_head(b, h):
                    m = known(sp, b * 2 + h + KD)
                    need = known(sp, at(b, 2, h + 1))
                    sp.wait_ge(y_r, need)
                    sp.dma_start(y_v[:, bass.ds(m, 1), :].rearrange("p m t -> p (m t)"), V[h][:]).then_inc(yh_st[h], 16)

                with sp.Fori(0, NB - 1) as b:
                    load_block(b, False)
                load_block(NB - 1, True)

                def load_w(i):
                    if i in (2, 3):
                        sp.wait_ge(wo_lo, i - 1)
                    elif i in (4, 5):
                        sp.wait_ge(y_r, at(NB, 2, 0))
                    elif i >= 6:
                        sp.wait_ge(wo_lo, i - 3)
                    slot = raw_slot(i)[0]
                    sp.dma_start(WR[slot][:], wo_v[order[i]]).then_inc(wr_land[slot], 16)

                def load_y(g, p):
                    m0, m1 = PIECES[p]
                    sp.dma_start(YR[p][:], y_g[:, g, m0:m1, :]).then_inc(yr_land[p], 16)

                def load_x(g, j):
                    sp.dma_start(XR[j][:], x_v[2 * g + j]).then_inc(xr_land[j], 16)

                sp.dma_start(pwo[:], post_norm_w.to_broadcast([P, D])).then_inc(pw2_land, 16)
                sp.wait_ge(pe_dg, at(NB, 2, 0))
                load_w(0)
                load_w(1)
                sp.wait_ge(x_r, at(NB, 16, 0))
                sp.wait_ge(pe_u, at(NB, 2, 0))
                sp.wait_ge(yl_st, at(NB - 1, 32, 0))
                load_y(0, 0)
                for h in range(2):
                    sp.wait_ge(yh_st[h], at(NB - 1, 16, 0))
                load_y(0, 1)
                sp.wait_ge(yl_st, at(NB, 32, 0))
                load_y(0, 2)
                load_w(2)
                load_w(3)
                store_head(NB - 1, 0)
                store_head(NB - 1, 1)
                for i in range(4, MT):
                    load_w(i)
                    if i == 5:
                        for h in range(2):
                            sp.wait_ge(yh_st[h], at(NB, 16, 0))
                        load_y(0, 3)
                sp.wait_ge(wo_lo, MT - 2)
                for j in range(2):
                    load_x(0, j)
                for n, (g, j, cols) in enumerate(PARTS):
                    if j == 0 and g + 1 < NG:
                        for p in range(NPC):
                            sp.wait_ge(yl2_r, g * NPC + p + 1)
                            load_y(g + 1, p)
                    sp.wait_ge(o2_done, n + 1)
                    sp.dma_start(o_v[2 * g + j][:, cols], OT[j][:, cols]).then_inc(out_st[j], 16)
                    if g + 1 < NG:
                        load_x(g + 1, j)
                sp.wait_ge(out_st[0], 16 * NG)
                sp.wait_ge(out_st[1], 16 * (NG + 1))

            @blk.gpsimd
            def _(pool):
                start_full(pool, PER_POOL)
                n = [0]

                def step(ins):
                    n[0] += 1
                    ins.then_inc(c_pool, 1)
                    pool.wait_ge(c_pool, n[0])

                step(pool.memset(ident[:], 0.0))
                step(pool.affine_select(out=ident[:], in_=ident[:], compare_op=ALU.not_equal, fill=1.0, base=0,
                                        pattern=[[-1, P]], channel_multiplier=1))
                step(pool.memset(eps_c[:], EPS))
                pool.wait_ge(w_land[0], 16)
                pool.tensor_copy(whi[0][:], wraw[0][:]).then_inc(w_hi0, 1)
                pool.wait_ge(w_hi0, 1)
                pool.tensor_tensor(wlo[0][:], wraw[0][:], whi[0][:], ALU.subtract).then_inc(w_lo, 1)
                def low_parts(b, ks, last=False):
                    for k in ks:
                        pool.wait_ge(w_hi, at(b, NS, k + 1))
                        pool.tensor_tensor(wlo[k % SLOTS][:], wraw[k % 2][:], whi[k % SLOTS][:],
                                           ALU.subtract).then_inc(w_lo, 1)
                        sec, j = SLABS[(k + 2) % NS]
                        if sec == SEC_X and not last:
                            pool.wait_ge(w_lo, at(b, NS, k + 1))
                            pool.dma_start(wraw[k % 2][:], w_v[:, :, sec, bass.ds(b * 2 + j + 2, 1), :].rearrange(
                                "p k j c -> p k (j c)")).then_inc(wx_land[j], 16)

                low_parts(0, range(1, 2))
                step(pool.memset(SG[:, 0:P], 1.0 / P))
                pool.tensor_copy(ones[:], SG[:, 0:P])
                pool.memset(mfl_c[:], M_FLOOR)
                pool.memset(S[:], 0.0)
                step(pool.memset(keep[:], 1))
                step(pool.memset(keep[:].rearrange("p (c t) -> p c t", t=P)[:, :, 0:1], 0))
                for l, m in maskl.items():
                    mm = m[:, 0]
                    step(pool.memset(m[:], 1))
                    step(pool.affine_select(out=mm, in_=mm, compare_op=ALU.is_ge, fill=0, base=0,
                                            pattern=[[-2 * l, P // (2 * l)], [0, l]], channel_multiplier=1))
                    step(pool.affine_select(out=mm, in_=mm, compare_op=ALU.is_ge, fill=0, base=l - 1,
                                            pattern=[[2 * l, P // (2 * l)], [0, l]], channel_multiplier=-1))
                md = maskd[:, 0].rearrange("p (i t) -> p i t", t=SUB)
                step(pool.memset(maskd[:], 1))
                step(pool.affine_select(out=md, in_=md, compare_op=ALU.is_ge, fill=0, base=0,
                                        pattern=[[-SUB, P // SUB], [0, SUB]], channel_multiplier=1))
                pool.affine_select(out=md, in_=md, compare_op=ALU.is_ge, fill=0, base=0,
                                   pattern=[[SUB, P // SUB], [1, SUB]], channel_multiplier=-1).then_inc(c_const, 1)

                low_parts(0, range(2, 3))
                with pool.Fori(0, NB - 1) as b:
                    low_parts(b, range(3, NS + 3))
                low_parts(NB - 1, range(3, NS), True)

            @blk.scalar
            def _(act):
                start_full(act, PER_ACT)
                act.sem_inc(w_hi, 1)
                A = nc.scalar.activation

                def high_part(b, k):
                    sec, j = SLABS[k % NS]
                    if k == 1:
                        act.wait_ge(w_land[1], 16)
                    elif sec == SEC_X:
                        act.wait_ge(wx_land[j], b * 16 + 16)
                    else:
                        before = sum(s % 2 == k % 2 and SLABS[s][0] != SEC_X for s in range(k % NS))
                        act.wait_ge(w_land[k % 2], (b + k // NS) * 80 + (before + 2) * 16)
                    act.wait_ge(slab, at(b, NS, k - 1 if SLABS[(k - 3) % NS] == (SEC_V, 0) else k - 2))
                    A(whi[k % SLOTS][:], wraw[k % 2][:], ACT.Copy).then_inc(w_hi, 1)

                loaded = [None]

                def table(name):
                    if loaded[0] != name:
                        loaded[0] = name
                        nc.scalar.preload_act_table_set(name)

                LOG_EXP, SIGMOID = "natural_log_exp_and_others", "sigmoid_and_others"
                table(LOG_EXP)

                def tile_rstd(t):
                    act.wait_ge(x_land[t], 16)
                    if t >= 1:
                        act.wait_ge(x_ssq, t)
                    A(Et[0][:], xstage[t][:], ACT.Square, accum_out=ssq[:, t:t + 1]).then_inc(x_ssq, 1)
                    act.wait_ge(x_ssq, t + 1)
                    act.wait_ge(c_pool, 3)
                    A(rst[:, t:t + 1], ssq[:, t:t + 1], ACT.Ln, scale=1.0 / D, bias=eps_c[:]).then_inc(x_ln, 1)
                    act.wait_ge(x_ln, t + 1)
                    A(rst[:, t:t + 1], rst[:, t:t + 1], ACT.Exp, scale=-0.5).then_inc(x_rst, 1)

                def tile_high(t):
                    act.wait_ge(x_tr, t + 1)
                    A(uhi[:, :, t * P:(t + 1) * P], chunks(mix[t % 2]), ACT.Copy).then_inc(u_hi, 1)

                def parameter_exps():
                    act.wait_ge(p_dve, 4)
                    A(der[:, TMP + 0], der[:, TMP + 0], ACT.Exp).then_inc(p_act, 1)
                    A(der[:, TMP + 1], der[:, TMP + 1], ACT.Exp).then_inc(p_act, 1)
                    A(der[:, TMP + 2], der[:, TMP + 2], ACT.Exp, scale=-1.0).then_inc(p_act, 1)

                tile_rstd(0); tile_rstd(1)
                for t in range(2, NT):
                    tile_high(t - 2)
                    tile_rstd(t)
                    if t == 3:
                        high_part(0, 1)
                    elif t == 6:
                        parameter_exps()
                tile_high(NT - 2)
                tile_high(NT - 1)
                high_part(0, 2)
                def forget_gate(b, h):
                    s = SLAB[SEC_F, h]
                    act.wait_ge(slab, at(b, NS, s + 1))
                    act.wait_ge(x_r, at(b, 16, 8 * h - 8))
                    if h == 1:
                        act.wait_ge(h_r, at(b, 2, 2))
                    A(K[h][:], prod[s % 2][:], ACT.Sigmoid).then_inc(sf_r, 1)

                def log_f(b, h):
                    act.wait_ge(sf_r, at(b, 2, h + 1))
                    act.wait_ge(e_r, at(b, 16, 8 * h))
                    A(Bs[:], K[h][:], ACT.Ln, scale=col(der, OML, b * 2 + h),
                      bias=col(der, LBC, b * 2 + h)).then_inc(lf_r, 1)

                def exps(b, h, n):
                    e = Et[(n - 1) % 2]
                    if n == 6:
                        act.wait_ge(b_r, at(b, 2, h + 1))
                    else:
                        act.wait_ge(d_r, at(b, 12, 6 * h + min(n, 6)))
                    act.wait_ge(x_r, at(b, 16, 8 * h + n - 2))
                    if 2 <= n <= 5:
                        l = LEVELS[n - 2]
                        dv, ev = chunks(Dt[(n - 1) % 2], 2 * l), chunks(e, 2 * l)
                        A(ev[:, :, 0:l], dv[:, :, 0:l], ACT.Exp, scale=-1.0)
                        A(ev[:, :, l:], dv[:, :, l:], ACT.Exp).then_inc(e_r, 1)
                    elif n == 6:
                        A(e[:], Bs[:], ACT.Exp).then_inc(e_r, 1)
                    else:
                        A(e[:], Dt[(min(n, 6) - 1) % 2][:], ACT.Exp, scale=1.0 if n == 7 else -1.0).then_inc(e_r, 1)

                def chunk_decay(b, h):
                    act.wait_ge(b_r, at(b, 2, h + 1))
                    act.wait_ge(st_r, at(b, 14, 7 * h))
                    A(dec[:], chunks(Bs)[:, :, P - 1], ACT.Exp).then_inc(dec_r, 1)

                def query_gate(b, h):
                    s = SLAB[SEC_Q, h]
                    act.wait_ge(slab, at(b, NS, s + 1))
                    act.wait_ge(y_r, at(b, 2, h - 1))
                    A(Q[h][:], prod[s % 2][:], ACT.Sigmoid).then_inc(sq_r, 1)

                def values(b, half):
                    sl = SLAB[SEC_V, half]
                    act.wait_ge(slab, at(b, NS, sl + 1))
                    for h in range(2):
                        act.wait_ge(yh_st[h], at(b, 16, 0))
                        last = A(chunks(V[h])[:, half * 4:half * 4 + 4],
                                 prod[sl % 2][:].rearrange("p (c h v) -> p h c v", h=2, v=P)[:, h], ACT.Copy)
                    last.then_inc(v_r, 1)

                def keys_by_token(b, h):
                    act.wait_ge(pe_tk, at(b, 2, h + 1))
                    A(KE[:], mix[0][:], ACT.Copy).then_inc(kt_r, 1)

                def gate_weights_high(b):
                    for g in range(2):
                        act.wait_ge(g_land[g], b * 16 + 16)
                    act.wait_ge(pe_o, at(b, 2, 0))
                    A(gwh[:], gw[:], ACT.Copy).then_inc(gwh_r, 1)

                def conv_high(b, i):
                    act.wait_ge(cv_r, at(b, 6, 3 * i + 3))
                    act.wait_ge(pe_dg, at(b, 2, 0))
                    A(xch[i][:], XC[i][:], ACT.Copy).then_inc(xh_r, 1)

                def square_out(b, h):
                    act.wait_ge(pe_o, at(b, 2, h + 1))
                    act.wait_ge(z_r, at(b, 2, h))
                    act.wait_ge(lu_r, at(b, 2, 2))
                    A(G[:], mix[0][:], ACT.Square).then_inc(o2_r, 1)
                    act.wait_ge(o2_r, at(b, 2, h + 1))
                    act.wait_ge(h_r, at(b, 2, 2))
                    act.wait_ge(pe_ms, at(b, 2, h))
                    A(o2h[:], G[:], ACT.Copy).then_inc(o2h_r, 1)

                def head_rstd(b, h):
                    act.wait_ge(pe_ms, at(b, 2, h + 1))
                    A(G[:], mix[1][:], ACT.Ln, bias=eps_c[:]).then_inc(ln_r, 1)
                    act.wait_ge(ln_r, at(b, 2, h + 1))
                    A(G[:], G[:], ACT.Exp, scale=-0.5).then_inc(rs_r, 1)

                def head_gate(b, h):
                    s = SLAB[SEC_HG, h]
                    act.wait_ge(slab, at(b, NS, s + 1))
                    act.wait_ge(pe_o, at(b, 2, h + 1))
                    A(V[h][:], prod[s % 2][:], ACT.Sigmoid).then_inc(shg_r, 1)

                def first_tap(b, i):
                    s = SLAB[SEC_X, i]
                    act.wait_ge(slab, at(b, NS, s + 1))
                    act.wait_ge(yl_r, at(b, 2, i - 1))
                    act.wait_ge(p_dve, 1)
                    A(XC[i][:], prod[s % 2][:], ACT.Identity, scale=col(par, CW + 3, b * 2 + i),
                      bias=col(par, CB, b * 2 + i)).then_inc(xt_r, 1)

                def lru_gates(b, i):
                    act.wait_ge(pe_g, at(b, 4, 2 * i + 1))
                    if i == 1:
                        act.wait_ge(x_r, at(b, 16, 0))
                        act.wait_ge(y_r, at(b, 2, 0))
                        act.wait_ge(pe_o, at(b, 2, 0))
                    A(Rg[i][:], mix[0][:], ACT.Sigmoid, bias=col(par, BA, b * 2 + i)).then_inc(r_r, 1)
                    act.wait_ge(pe_g, at(b, 4, 2 * i + 2))
                    A(Ig[i][:], mix[1][:], ACT.Sigmoid, bias=col(par, BX, b * 2 + i)).then_inc(i_r, 1)
                    act.wait_ge(r_r, at(b, 2, i + 1))
                    act.wait_ge(z_r, at(b, 2, 0))
                    act.wait_ge(p_par, 1)
                    A(Gg[i][:], Rg[i][:], ACT.Tanh, scale=col(der, C8, b * 2 + i)).then_inc(th_r, 1)

                def lru_decay(b, i):
                    act.wait_ge(th_r, at(b, 2, i + 1))
                    A(Rg[i][:], Rg[i][:], ACT.Exp, scale=col(der, NC8, b * 2 + i)).then_inc(a_r, 1)
                    act.wait_ge(a_r, at(b, 2, i + 1))
                    if i == 0:
                        act.wait_ge(yl_st, at(b, 32, 0))
                    else:
                        act.wait_ge(m2_r, at(b, 2, 1))
                    A(SG[:], Rg[i][:], ACT.Square).then_inc(a2_r, 1)

                def lru_input(b, i):
                    act.wait_ge(m2_r, at(b, 2, i + 1))
                    A(Gg[i][:], Gg[i][:], ACT.Ln, bias=mfl_c[:]).then_inc(ml_r, 1)
                    act.wait_ge(ml_r, at(b, 2, i + 1))
                    A(Gg[i][:], Gg[i][:], ACT.Exp, scale=0.5).then_inc(m_r, 1)

                def lru_gate(b, i):
                    s = SLAB[SEC_LG, i]
                    act.wait_ge(slab, at(b, NS, s + 1))
                    if i == 0:
                        act.wait_ge(m2_r, at(b, 2, 2))
                    else:
                        act.wait_ge(yl_st, at(b, 32, 16))
                    A(SG[:], prod[s % 2][:], ACT.Sigmoid).then_inc(slg_r, 1)

                def store_lru(b, i):
                    m = known(act, b * 2 + i)
                    act.wait_ge(yl_r, at(b, 2, i + 1))
                    act.dma_start(y_v[:, bass.ds(m, 1), :].rearrange("p m t -> p (m t)"), SG[:]).then_inc(yl_st, 16)

                def y_high(g, p):
                    act.wait_ge(yr_land[p], 16 * (g + 1))
                    if g == 0:
                        act.wait_ge(yl_r, at(NB, 2, 0))
                        act.wait_ge(x_r, at(NB, 16, 0))
                    else:
                        act.wait_ge(*piece_used(g - 1, p))
                    A(YH[p][:], YR[p][:], ACT.Copy).then_inc(yh_r, 1)

                def w_high(i):
                    slot, nth = raw_slot(i)
                    act.wait_ge(wr_land[slot], 16 * nth)
                    if i < 2:
                        act.wait_ge(pe_dg, at(NB, 2, 0))
                    else:
                        act.wait_ge(slab, at(NB, NS, 0))
                    A(wo_part(0, i), WR[slot][:], ACT.Copy).then_inc(wo_hi, 1)

                def out_rstd(n):
                    g, j, cols = PARTS[n]
                    c = 2 * g + j
                    act.wait_ge(pe_part, n + 1)
                    act.wait_ge(wo_lo, MT)
                    if n >= 2:
                        act.wait_ge(sq2_r, n - 1)
                    A(WR[n % 2][:, cols], acc[g % 2][j][:, cols], ACT.Square, accum_out=ssq[:, n:n + 1]).then_inc(sq2_r, 1)
                    act.wait_ge(sq2_r, n + 1)
                    if n == len(PARTS) - 2:
                        A(eps2[:], ssq[:, n:n + 1], ACT.Identity, scale=1.0 / D, bias=eps_c[:]).then_inc(eb_r, 1)
                        return
                    if n == len(PARTS) - 1:
                        act.wait_ge(eb_r, 1)
                    A(rst[:, c:c + 1], ssq[:, n:n + 1], ACT.Ln, scale=1.0 / D,
                      bias=(eps2 if n == len(PARTS) - 1 else eps_c)[:]).then_inc(ln2_r, 1)
                    act.wait_ge(ln2_r, c + 1)
                    A(rst[:, c:c + 1], rst[:, c:c + 1], ACT.Exp, scale=-0.5).then_inc(rs2_r, 1)

                def block_act(b, last):
                    loaded[0] = None
                    gate_weights_high(b)
                    first_tap(b, 0); high_part(b, 3)
                    conv_high(b, 0)
                    first_tap(b, 1); high_part(b, 4)
                    conv_high(b, 1)
                    table(SIGMOID)
                    lru_gates(b, 0)
                    forget_gate(b, 0)
                    lru_gates(b, 1)
                    high_part(b, 5)
                    table(LOG_EXP)
                    log_f(b, 0)
                    lru_decay(b, 0)
                    exps(b, 0, 1); exps(b, 0, 2); chunk_decay(b, 0)
                    lru_decay(b, 1)
                    lru_input(b, 0)
                    table(SIGMOID)
                    query_gate(b, 0); high_part(b, 6)
                    table(LOG_EXP)
                    lru_input(b, 1)
                    exps(b, 0, 3)
                    keys_by_token(b, 0)
                    exps(b, 0, 4)
                    values(b, 0)
                    exps(b, 0, 5); exps(b, 0, 6); exps(b, 0, 7); exps(b, 0, 8)
                    values(b, 1); high_part(b, 7); high_part(b, 8)
                    table(SIGMOID)
                    forget_gate(b, 1); high_part(b, 9)
                    table(LOG_EXP)
                    log_f(b, 1)
                    square_out(b, 0)
                    exps(b, 1, 1)
                    head_rstd(b, 0)
                    exps(b, 1, 2); chunk_decay(b, 1)
                    table(SIGMOID)
                    query_gate(b, 1); high_part(b, 10)
                    table(LOG_EXP)
                    exps(b, 1, 3)
                    keys_by_token(b, 1)
                    exps(b, 1, 4)
                    exps(b, 1, 5); exps(b, 1, 6); exps(b, 1, 7); exps(b, 1, 8)
                    table(SIGMOID)
                    lru_gate(b, 0); high_part(b, 11)
                    store_lru(b, 0)
                    lru_gate(b, 1)
                    if not last:
                        high_part(b, 12)
                    store_lru(b, 1)
                    square_out(b, 1)
                    if last:
                        w_high(0)
                        w_high(1)
                        y_high(0, 0)
                    head_gate(b, 0)
                    if not last:
                        high_part(b, 13)
                    table(LOG_EXP)
                    head_rstd(b, 1)
                    table(SIGMOID)
                    head_gate(b, 1)
                    if not last:
                        high_part(b, 14)

                with act.Fori(0, NB - 1) as b:
                    block_act(b, False)
                block_act(NB - 1, True)
                for i in range(2, MT):
                    w_high(i)
                    if i in (3, 6, 9):
                        y_high(0, i // 3)
                table(LOG_EXP)
                for n, (g, j, cols) in enumerate(PARTS):
                    if j == 0 and g + 1 < NG:
                        for p in range(NPC - 1):
                            y_high(g + 1, p)
                    out_rstd(n)
                    if j == 1 and g + 1 < NG:
                        y_high(g + 1, NPC - 1)

            @blk.vector
            def _(dve):
                start_full(dve, PER_DVE)
                V_ = nc.vector
                TT, TS, STT = V_.tensor_tensor, V_.tensor_scalar, V_.scalar_tensor_tensor

                def tile_scaled(t):
                    if t == 0:
                        dve.wait_ge(pw_land, 16)
                    dve.wait_ge(x_rst, t + 1)
                    STT(out=xstage[t][:], in0=xstage[t][:], scalar=rst[:, t:t + 1], in1=pwb[:],
                        op0=ALU.mult, op1=ALU.mult).then_inc(x_scaled, 1)

                def tile_low(t):
                    dve.wait_ge(u_hi, t + 1)
                    tok = slice(t * P, (t + 1) * P)
                    TT(ulo[:, :, tok], chunks(mix[t % 2]), uhi[:, :, tok], ALU.subtract).then_inc(u_lo, 1)

                n = [0]

                def step(ins):
                    n[0] += 1
                    ins.then_inc(p_dve, 1)
                    dve.wait_ge(p_dve, n[0])

                def tmp(i):
                    return der[:, TMP + i]

                def exp_operands():
                    TT(tmp(3), par[:, LB0], par[:, LB1], ALU.max).then_inc(p_dve, 1)
                    n[0] += 1
                    step(TS(tmp(4), par[:, LAM], -1.0, None, ALU.mult))
                    TT(tmp(0), par[:, LB0], tmp(3), ALU.subtract)
                    TT(tmp(1), par[:, LB1], tmp(3), ALU.subtract)
                    step(TT(tmp(2), par[:, LAM], tmp(4), ALU.max))

                def lower_bounds():
                    dve.wait_ge(p_act, 3)
                    step(TT(tmp(3), tmp(0), tmp(1), ALU.add))
                    step(V_.reciprocal(tmp(3), tmp(3)))
                    TT(der[:, LBC], tmp(0), tmp(3), ALU.mult)
                    step(TT(der[:, OML], tmp(1), tmp(3), ALU.mult))
                    step(TS(der[:, LBC], der[:, LBC], F_FLOOR, None, ALU.max))
                    step(TS(der[:, NOML], der[:, OML], -1.0, None, ALU.mult))
                    step(TS(tmp(5), tmp(2), 2.0, None, ALU.add))
                    step(V_.reciprocal(tmp(5), tmp(5)))
                    step(TT(tmp(5), tmp(5), tmp(2), ALU.mult))
                    step(TT(tmp(6), tmp(5), tmp(5), ALU.mult))
                    step(TS(tmp(7), tmp(6), 1.0 / 19, 1.0 / 17, ALU.mult, ALU.add))

                def lru_constants():
                    for k in range(15, 0, -2):
                        step(TT(tmp(7), tmp(7), tmp(6), ALU.mult))
                        step(TS(tmp(7), tmp(7), 1.0 / k, None, ALU.add))
                    step(TT(tmp(7), tmp(7), tmp(5), ALU.mult))
                    step(TS(tmp(4), tmp(4), 0.0, LRU_C, ALU.max, ALU.mult))
                    step(STT(out=der[:, C8], in0=tmp(7), scalar=2.0 * LRU_C, in1=tmp(4), op0=ALU.mult, op1=ALU.add))
                    step(TS(der[:, NC8], der[:, C8], -1.0, None, ALU.mult))
                    dve.wait_ge(c_const, 1)
                    V_.memset(gate[:], 0.0).then_inc(p_par, 1)

                tile_scaled(0); tile_scaled(1)
                for t in range(2, NT):
                    tile_low(t - 2)
                    tile_scaled(t)
                    if t == 4:
                        dve.wait_ge(p_T, 1)
                        step(V_.tensor_copy(par[:], prod[1][:, HALF:HALF + NPAR * KD].rearrange("p (r j) -> p r j", j=KD)))
                        exp_operands()
                tile_low(NT - 2)
                lower_bounds()
                tile_low(NT - 1)
                lru_constants()

                def key(b, h):
                    dve.wait_ge(lf_r, at(b, 2, h + 1))
                    TS(K[h][:], K[h][:], col(der, NOML, b * 2 + h), col(der, OML, b * 2 + h),
                       ALU.mult, ALU.add).then_inc(k_r, 1)
                    V_.tensor_tensor_scan(Bs[:], keep[:], Bs[:], 0.0, ALU.mult, ALU.add).then_inc(b_r, 1)

                def diff(b, h, j):
                    w, ref = {1: (P, P - 1), 6: (SUB, SUB // 2 - 1)}.get(j) or (2 * LEVELS[j - 2], LEVELS[j - 2] - 1)
                    dve.wait_ge(b_r, at(b, 2, h + 1))
                    dve.wait_ge(e_r, at(b, 16, 8 * h + {1: -3, 2: 0}.get(j, j - 2)))
                    bv = chunks(Bs, w)
                    TT(chunks(Dt[(j - 1) % 2], w), bv, bv[:, :, ref:ref + 1].to_broadcast([P, T // w, w]),
                       ALU.subtract).then_inc(d_r, 1)

                def prod_e(b, h, n):
                    e = Et[(n - 1) % 2]
                    dve.wait_ge(e_r, at(b, 16, 8 * h + n))
                    if n == 1:
                        dve.wait_ge(k_r, at(b, 2, h + 1))
                        dve.wait_ge(pe_u, at(b, 2, h))
                        TT(KE[:], K[h][:], e[:], ALU.mult).then_inc(x_r, 1)
                    elif n <= 5:
                        l = LEVELS[n - 2]
                        dve.wait_ge(q_r, at(b, 2, h + 1))
                        dve.wait_ge(pe_dg, at(b, 2, h))
                        dve.wait_ge(pe_g, at(b, 4, 4))
                        xv, ev = chunks(X4[n - 2], 2 * l), chunks(e, 2 * l)
                        TT(xv[:, :, 0:l], chunks(K[h], 2 * l)[:, :, 0:l], ev[:, :, 0:l], ALU.mult)
                        TT(xv[:, :, l:], chunks(Q[h], 2 * l)[:, :, l:], ev[:, :, l:], ALU.mult).then_inc(x_r, 1)
                    elif n == 6:
                        dve.wait_ge(pe_o, at(b, 2, h))
                        TT(QE[:], Q[h][:], e[:], ALU.mult).then_inc(x_r, 1)
                    else:
                        dve.wait_ge(pe_l, at(b, 8, 4 * h + n - 6))
                        TT(X4[n - 7][:], (Q, K)[n - 7][h][:], e[:], ALU.mult).then_inc(x_r, 1)

                def query(b, h):
                    dve.wait_ge(sq_r, at(b, 2, h + 1))
                    TT(Q[h][:], Q[h][:], prod[SLAB[SEC_Q, h] % 2][:], ALU.mult).then_inc(q_r, 1)

                def states(b, h):
                    dve.wait_ge(pe_u, at(b, 2, h + 1))
                    dve.wait_ge(pe_o, at(b, 2, h))
                    dve.wait_ge(dec_r, at(b, 2, h + 1))
                    V_.tensor_copy(ST[:, 1], mix[0][:, 0:P]).then_inc(st_r, 1)
                    for c in range(1, NC - 1):
                        dve.wait_ge(st_r, at(b, 14, 7 * h + c))
                        STT(out=ST[:, c + 1], in0=ST[:, c], scalar=dec[:, c:c + 1], in1=mix[0][:, c * P:(c + 1) * P],
                            op0=ALU.mult, op1=ALU.add).then_inc(st_r, 1)

                def scores(b, h, i):
                    dve.wait_ge(sc_r, at(b, 10, 5 * h + i))
                    if i == 0:
                        dve.wait_ge(pe_o, at(b, 2, h))
                    if i < 4:
                        dve.wait_ge(pe_l, at(b, 8, 4 * h + i + 1))
                    else:
                        dve.wait_ge(pe_dg, at(b, 2, h + 1))
                    V_.memset(gate[:], 0.0)
                    m = mix[(1, 0, 1, 0, 1)[i]]
                    if i == 0:
                        l = LEVELS[0]
                        V_.tensor_copy(S[0:l, :, l:], m[0:l, 0:HALF].rearrange("p (c t) -> p c t", t=l)).then_inc(sc_r, 1)
                    elif i < 4:
                        l = LEVELS[i]
                        nb = P // (2 * l)
                        V_.copy_predicated(S[0:P - l].rearrange("p c (i t) -> p c i t", t=2 * l)[:, :, :, l:],
                                           maskl[l][0:P - l].to_broadcast([P - l, NC, nb, l]),
                                           m[0:P - l, 0:HALF].rearrange("p (c i t) -> p c i t", c=NC, t=l)
                                           ).then_inc(sc_r, 1)
                    else:
                        V_.copy_predicated(S[:], maskd[:].to_broadcast([P, NC, P]), chunks(m)).then_inc(sc_r, 1)

                def norm(b, h):
                    dve.wait_ge(rs_r, at(b, 2, h + 1))
                    dve.wait_ge(x_r, at(b, 16, 8 * h + 8))
                    STT(out=Q[h][:], in0=mix[0][:], scalar=col(par, GN, b * 2 + h), in1=G[:],
                        op0=ALU.mult, op1=ALU.mult).then_inc(z_r, 1)

                def gate_out(b, h):
                    dve.wait_ge(shg_r, at(b, 2, h + 1))
                    TT(V[h][:], V[h][:], prod[SLAB[SEC_HG, h] % 2][:], ALU.mult).then_inc(hg_r, 1)

                def head_out(b, h):
                    dve.wait_ge(hg_r, at(b, 2, h + 1))
                    dve.wait_ge(z_r, at(b, 2, h + 1))
                    TT(V[h][:], V[h][:], Q[h][:], ALU.mult).then_inc(y_r, 1)

                def conv(b, i):
                    dve.wait_ge(xt_r, at(b, 2, i + 1))
                    src = prod[SLAB[SEC_X, i] % 2]
                    for d in range(1, 4):
                        if d > 1:
                            dve.wait_ge(cv_r, at(b, 6, 3 * i + d - 1))
                        STT(out=XC[i][:, d:], in0=src[:, 0:T - d], scalar=col(par, CW + 3 - d, b * 2 + i),
                            in1=XC[i][:, d:], op0=ALU.mult, op1=ALU.add).then_inc(cv_r, 1)

                def gate_weights_low(b):
                    dve.wait_ge(gwh_r, at(b, 1, 1))
                    dve.wait_ge(pe_o, at(b, 2, 0))
                    TT(gwl[:], gw[:], gwh[:], ALU.subtract).then_inc(gwl_r, 1)

                def conv_low(b, i):
                    dve.wait_ge(xh_r, at(b, 2, i + 1))
                    dve.wait_ge(pe_l, at(b, 8, 0))
                    TT(xcl[i][:], XC[i][:], xch[i][:], ALU.subtract).then_inc(xl_r, 1)

                def square_low(b, h):
                    dve.wait_ge(o2h_r, at(b, 2, h + 1))
                    dve.wait_ge(pe_ms, at(b, 2, h))
                    TT(o2l[:], G[:], o2h[:], ALU.subtract).then_inc(o2l_r, 1)

                def gated_input(b, i):
                    dve.wait_ge(i_r, at(b, 2, i + 1))
                    TT(Ig[i][:], Ig[i][:], XC[i][:], ALU.mult).then_inc(ix_r, 1)

                def lru_factor(b, i):
                    dve.wait_ge(a2_r, at(b, 2, i + 1))
                    STT(out=Gg[i][:], in0=SG[:], scalar=1.0, in1=Gg[i][:], op0=ALU.add, op1=ALU.mult).then_inc(m2_r, 1)

                def lru_scan(b, i):
                    dve.wait_ge(m_r, at(b, 2, i + 1))
                    dve.wait_ge(ix_r, at(b, 2, i + 1))
                    TT(Ig[i][:], Ig[i][:], Gg[i][:], ALU.mult).then_inc(lu_r, 1)
                    dve.wait_ge(lu_r, at(b, 2, i + 1))
                    dve.wait_ge(xh_r, at(b, 2, i + 1))
                    V_.tensor_tensor_scan(XC[i][:], Rg[i][:], Ig[i][:], 0.0, ALU.mult, ALU.add).then_inc(h_r, 1)

                def lru_out(b, i):
                    dve.wait_ge(slg_r, at(b, 2, i + 1))
                    TT(SG[:], SG[:], prod[SLAB[SEC_LG, i] % 2][:], ALU.mult).then_inc(lg_r, 1)
                    dve.wait_ge(lg_r, at(b, 2, i + 1))
                    dve.wait_ge(h_r, at(b, 2, i + 1))
                    TT(SG[:], SG[:], XC[i][:], ALU.mult).then_inc(yl_r, 1)

                def y_low(g, p):
                    dve.wait_ge(yh_r, g * NPC + p + 1)
                    if g == 0:
                        dve.wait_ge(e_r, at(NB, 16, 0))
                        dve.wait_ge(pe_o, at(NB, 2, 0))
                    else:
                        dve.wait_ge(*piece_used(g - 1, p))
                    TT(YL[p][:], YR[p][:], YH[p][:], ALU.subtract).then_inc(yl2_r, 1)

                def w_low(i):
                    dve.wait_ge(wo_hi, i + 1)
                    if i < 2:
                        dve.wait_ge(e_r, at(NB, 16, 0))
                    else:
                        dve.wait_ge(slab, at(NB, NS, 0))
                    TT(wo_part(1, i), WR[raw_slot(i)[0]][:], wo_part(0, i), ALU.subtract).then_inc(wo_lo, 1)

                def weigh(n):
                    g, j, cols = PARTS[n]
                    dve.wait_ge(sq2_r, n + 1)
                    dve.wait_ge(pw2_land, 16)
                    if g == 0:
                        dve.wait_ge(yh_st[j], at(NB, 16, 0))
                    else:
                        dve.wait_ge(out_st[j], 16 * g)
                    TT(OT[j][:, cols], acc[g % 2][j][:, cols], pwo[:, cols], ALU.mult).then_inc(o1_r, 1)

                def finish(n):
                    g, j, cols = PARTS[n]
                    dve.wait_ge(o1_r, n + 1)
                    dve.wait_ge(rs2_r, 2 * g + j + 1)
                    dve.wait_ge(xr_land[j], 16 * (g + 1))
                    STT(out=OT[j][:, cols], in0=OT[j][:, cols], scalar=rst[:, 2 * g + j:2 * g + j + 1], in1=XR[j][:, cols],
                        op0=ALU.mult, op1=ALU.add).then_inc(o2_done, 1)

                def block_dve(b, last):
                    conv(b, 0); conv_low(b, 0)
                    gate_weights_low(b)
                    conv(b, 1); conv_low(b, 1)
                    gated_input(b, 0)
                    gated_input(b, 1)
                    key(b, 0); diff(b, 0, 1); diff(b, 0, 2)
                    lru_factor(b, 0)
                    prod_e(b, 0, 1)
                    lru_factor(b, 1)
                    diff(b, 0, 3)
                    lru_scan(b, 0)
                    query(b, 0)
                    prod_e(b, 0, 2)
                    diff(b, 0, 4); prod_e(b, 0, 3)
                    lru_scan(b, 1)
                    diff(b, 0, 5); prod_e(b, 0, 4)
                    diff(b, 0, 6); prod_e(b, 0, 5)
                    prod_e(b, 0, 6)
                    scores(b, 0, 0); prod_e(b, 0, 7)
                    scores(b, 0, 1); prod_e(b, 0, 8)
                    scores(b, 0, 2)
                    scores(b, 0, 3)
                    scores(b, 0, 4)
                    states(b, 0)
                    key(b, 1); diff(b, 1, 1); diff(b, 1, 2)
                    square_low(b, 0)
                    prod_e(b, 1, 1)
                    norm(b, 0)
                    diff(b, 1, 3)
                    query(b, 1)
                    prod_e(b, 1, 2)
                    diff(b, 1, 4); prod_e(b, 1, 3)
                    diff(b, 1, 5); prod_e(b, 1, 4)
                    diff(b, 1, 6); prod_e(b, 1, 5)
                    prod_e(b, 1, 6)
                    scores(b, 1, 0); prod_e(b, 1, 7)
                    scores(b, 1, 1); prod_e(b, 1, 8)
                    lru_out(b, 0)
                    scores(b, 1, 2)
                    scores(b, 1, 3)
                    scores(b, 1, 4)
                    states(b, 1)
                    lru_out(b, 1)
                    square_low(b, 1)
                    if last:
                        w_low(0)
                        w_low(1)
                        y_low(0, 0)
                    gate_out(b, 0)
                    norm(b, 1)
                    head_out(b, 0)
                    gate_out(b, 1)
                    head_out(b, 1)

                with dve.Fori(0, NB - 1) as b:
                    block_dve(b, False)
                block_dve(NB - 1, True)
                for i in range(2, MT):
                    w_low(i)
                    if i in (3, 6, 9):
                        y_low(0, i // 3)
                for n, (g, j, cols) in enumerate(PARTS):
                    if j == 0 and g + 1 < NG:
                        for p in range(NPC - 1):
                            y_low(g + 1, p)
                    weigh(n)
                    if n == len(PARTS) - 2:
                        continue
                    if n == len(PARTS) - 1:
                        finish(n - 1)
                    finish(n)
                    if j == 1 and g + 1 < NG:
                        y_low(g + 1, NPC - 1)

            @blk.tensor
            def _(pe):
                start_full(pe, PER_PE)
                M = nc.tensor.matmul

                pe.wait_ge(c_pool, 2)

                def tile_transposed(t):
                    pe.wait_ge(x_scaled, t + 1)
                    if t >= 2:
                        pe.wait_ge(u_lo, t - 1)
                    for k in range(KD):
                        ks = slice(k * P, (k + 1) * P)
                        last = nc.tensor.transpose(mix[t % 2][:, ks], xstage[t][:, ks], ident[:])
                    last.then_inc(x_tr, 1)

                tile_transposed(0)
                tile_transposed(1)

                frees = {SEC_F: (sf_r, 2, 1), SEC_Q: (q_r, 2, 1), SEC_V: (v_r, 2, 1), SEC_X: (cv_r, 6, 3),
                         SEC_HG: (hg_r, 2, 1), SEC_LG: (lg_r, 2, 1)}

                def part_product(s, tok, behind):
                    hi, lo = whi[s % SLOTS], wlo[s % SLOTS]
                    n = 0
                    for k in range(KD):
                        for w, u in ((hi, uhi), (hi, ulo), (lo, uhi)):
                            last = M(prod[s % 2][:, tok], w[:, k], u[:, k, tok], start=(n == 0), stop=(n == 23))
                            n += 1
                        if k == KD - 1 and tok.stop == T:
                            last.then_inc(slab, 1)
                        behind(k)

                def values_product(b, s):
                    s0 = SLAB[SEC_V, 0] % SLOTS
                    hi, lo = [w[:, s0:s0 + 2] for w in w_split]
                    for i in range(NC // 2):
                        c = SLABS[s][1] * (NC // 2) + i
                        tok = slice(c * P, (c + 1) * P)
                        n = 0
                        for k in range(KD):
                            for u, w in ((uhi, hi), (uhi, lo), (ulo, hi)):
                                last = M(prod[s % 2][:, i * 2 * P:(i + 1) * 2 * P], u[:, k, tok], w[:, :, k],
                                         start=(n == 0), stop=(n == 23))
                                n += 1
                        if i == NC // 2 - 1:
                            last.then_inc(slab, 1)
                        for name, arg in WHEN.get(4 * s + i, []):
                            step(b, name, arg)

                def product(b, s):
                    pe.wait_ge(w_lo, at(b, NS, s + (2 if SLABS[s] == (SEC_V, 0) else 1)))
                    sec, j = SLABS[s - 2]
                    fs, per, each = frees[sec]
                    pe.wait_ge(fs, at(b, per, each * (j + 1) - (per if s < 2 else 0)))

                    if SLABS[s][0] == SEC_V:
                        values_product(b, s)
                        return
                    for half in range(2):
                        def behind(k):
                            if k % 4 == 3:
                                for name, arg in WHEN.get(4 * s + 2 * half + k // 4, []):
                                    step(b, name, arg)

                        part_product(s, slice(half * HALF, (half + 1) * HALF), behind)

                def step(b, name, h):
                    c_ = [slice(c * P, (c + 1) * P) for c in range(NC)]
                    if name == "tk":
                        pe.wait_ge(x_r, at(b, 16, 8 * h + 1))
                        pe.wait_ge(*((r_r, at(b, 2, 2)) if h == 0 else (z_r, at(b, 2, 1))))
                        for c in range(NC):
                            last = nc.tensor.transpose(mix[0][:, c_[c]], KE[:, c_[c]], ident[:])
                        last.then_inc(pe_tk, 1)
                    elif name == "u":
                        pe.wait_ge(kt_r, at(b, 2, h + 1))
                        pe.wait_ge(v_r, at(b, 2, 2))
                        pe.wait_ge(sc_r, at(b, 10, 5 * h + 4))
                        for c in range(NC - 1):
                            last = M(mix[0][:, c_[c]], KE[:, c_[c]], V[h][:, c_[c]], start=True, stop=True)
                        last.then_inc(pe_u, 1)
                    elif name[0] == "l":
                        i = int(name[1])
                        l = LEVELS[i]
                        pe.wait_ge(x_r, at(b, 16, 8 * h + 2 + i))
                        pe.wait_ge(*((i_r, at(b, 2, 2)) if h == 0 else (ln_r, at(b, 2, 1)), (kt_r, at(b, 2, h + 1)),
                                     (sc_r, at(b, 10, 5 * h + 1)), (sc_r, at(b, 10, 5 * h + 2)))[i])
                        for c in range(NC):
                            second = X4[i][:, c_[c]].rearrange("p (i t) -> p i t", t=2 * l)[:, :, l:]
                            keys = P - l
                            last = M(mix[(1, 0, 1, 0)[i]][0:keys, c * 64:(c + 1) * 64],
                                     X4[i][:, c * P:c * P + keys], second, start=True, stop=True)
                        last.then_inc(pe_l, 1)
                    elif name == "dg":
                        pe.wait_ge(x_r, at(b, 16, 8 * h + 8))
                        pe.wait_ge(sc_r, at(b, 10, 5 * h + 3))
                        for c in range(NC):
                            last = M(mix[1][:, c_[c]], X4[1][:, c_[c]], X4[0][:, c_[c]], start=True, stop=True)
                        last.then_inc(pe_dg, 1)
                    elif name == "o":
                        pe.wait_ge(x_r, at(b, 16, 8 * h + 6))
                        pe.wait_ge(sc_r, at(b, 10, 5 * h + 5))
                        pe.wait_ge(st_r, at(b, 14, 7 * (h + 1)))
                        for c in range(NC):
                            last = M(mix[0][:, c_[c]], V[h][:, c_[c]], S[:, c], start=True, stop=(c == 0))
                            if c:
                                last = M(mix[0][:, c_[c]], ST[:, c], QE[:, c_[c]], start=False, stop=True)
                        last.then_inc(pe_o, 1)
                    elif name == "ms":
                        pe.wait_ge(o2l_r, at(b, 2, h + 1))
                        for half in range(2):
                            t = slice(half * HALF, (half + 1) * HALF)
                            M(mix[1][:, t], ones[:], o2h[:, t], start=True, stop=False)
                            last = M(mix[1][:, t], ones[:], o2l[:, t], start=False, stop=True)
                        last.then_inc(pe_ms, 1)
                    elif name == "g":
                        i, gate_ = h // 2, h % 2
                        pe.wait_ge(gwl_r, at(b, 1, 1))
                        pe.wait_ge(xl_r, at(b, 2, 2))
                        pe.wait_ge(*((z_r, at(b, 2, 0)), (ln_r, at(b, 2, 0)), (r_r, at(b, 2, 1)), (i_r, at(b, 2, 1)))[h])
                        for half in range(2):
                            t = slice(half * HALF, (half + 1) * HALF)
                            for k in range(2):
                                for n, (w, xc) in enumerate(((gwh, xch), (gwl, xch), (gwh, xcl))):
                                    last = M(mix[h % 2][:, t], w[:, gate_, k, i * P:(i + 1) * P], xc[k][:, t],
                                             start=(k == 0 and n == 0), stop=(k == 1 and n == 2))
                        last.then_inc(pe_g, 1)

                tile_transposed(2)
                for i, (s, quarter) in enumerate([(0, 0), (1, 0), (0, 1), (1, 1), (0, 2), (0, 3), (1, 2), (1, 3)]):
                    pe.wait_ge(w_lo, at(0, NS, s + 1))
                    pe.wait_ge(u_lo, 2 * quarter + 2)
                    if (s, quarter) == (1, 2):
                        pe.wait_ge(p_dve, 1)

                    def behind(k):
                        t = {(0, 3): 3, (1, 1): 4, (2, 1): 5, (3, 0): 6, (3, 7): 7}.get((i, k))
                        if t is not None:
                            tile_transposed(t)
                        if (i, k) == (0, 7):
                            n = NPAR * KD
                            pe.wait_ge(p_land, 16 * 7)
                            nc.tensor.transpose(prod[1][:, HALF:HALF + n], prow[0:n, 0:P], ident[0:n, 0:n]).then_inc(p_T, 1)

                    part_product(s, slice(quarter * 2 * P, (quarter + 1) * 2 * P), behind)
                for s in range(2, NS):
                    product(0, s)
                with pe.Fori(1, NB - 1) as b:
                    for s in range(NS):
                        product(b, s)
                for s in range(NS):
                    product(NB - 1, s)

                def sums(g, p, i, m, j, halves, first, last_m):
                    tok = slice(j * P, (j + 1) * P)
                    for n, (y, w) in enumerate(((YH, 0), (YH, 1), (YL, 0))):
                        for half in halves:
                            d = slice(half * HALF, (half + 1) * HALF)
                            last = M(acc[g % 2][j][:, d], y[p][:, m, tok], wo_part(w, i)[:, d],
                                     start=(first and n == 0), stop=(last_m and n == 2))
                    return last

                tiles = [(i, p, i - sum(size[:p])) for i, p in enumerate(sum(([p] * size[p] for p in range(NPC)), []))]
                for g in range(NG):
                    if g == 0:
                        pe.wait_ge(hg_r, at(NB, 2, -1))
                        pe.wait_ge(ln_r, at(NB, 2, 0))
                    elif g == 1:
                        pe.wait_ge(z_r, at(NB, 2, 0))
                        pe.wait_ge(hg_r, at(NB, 2, 0))
                    else:
                        pe.wait_ge(o1_r, 2 * (g - 1))
                        pe.wait_ge(sq2_r, 2 * (g - 1))
                    if g < NG - 1:
                        for i, p, m in tiles:
                            if m == 0:
                                pe.wait_ge(yl2_r, g * NPC + p + 1)
                            if g == 0:
                                pe.wait_ge(wo_lo, i + 1)
                            for j in range(2):
                                last = sums(g, p, i, m, j, range(2), i == 0, i == MT - 1)
                                if i == MT - 1:
                                    last.then_inc(pe_part, 1)
                            if m == size[p] - 1 and i < MT - 1:
                                last.then_inc(pe_pc, 1)
                    else:
                        for j, halves in ((0, range(2)), (1, (0,)), (1, (1,))):
                            for i, p, m in tiles:
                                if m == 0:
                                    pe.wait_ge(yl2_r, g * NPC + p + 1)
                                last = sums(g, p, i, m, j, halves, i == 0, i == MT - 1)
                            last.then_inc(pe_part, 1)


INS = ["x", "pre_norm_w", "w_in", "conv_w", "conv_b", "lru_w_a", "lru_b_a", "lru_w_x", "lru_b_x", "lru_lambda",
       "hgrn_lb_logits", "hgrn_gnorm_w", "w_out", "post_norm_w"]


def kernel(**inputs):
    import numpy as np
    import concourse.bacc as bacc
    from concourse.bass_utils import run_bass_kernel_spmd

    nc = bacc.Bacc("TRN2", target_bir_lowering=False, num_devices=1)
    arrays, args = {}, []
    for name in INS:
        a = np.ascontiguousarray(inputs[name])
        arrays[f"in_{name}"] = a
        args.append(nc.dram_tensor(f"in_{name}", a.shape, mybir.dt.from_np(a.dtype), kind="ExternalInput").ap())
    _, seq, width = inputs["x"].shape
    out = nc.dram_tensor("out_h", (1, seq, width), F32, kind="ExternalOutput").ap()
    scratch = nc.dram_tensor("mixed", (inputs["w_out"].shape[1] // P, P, seq), F32, kind="Internal").ap()
    build(nc, *args, out, scratch)
    r = run_bass_kernel_spmd(nc, [arrays], core_ids=[0])
    return r.results[0]["out_h"]
```
